# Optimizing a Trainium2 kernel written in Bass

```python
import math, functools
import jax, jax.numpy as jnp
from jax import lax
import numpy as np

D_MODEL = 1024
BATCH = 1
SEQ = 256
DEPTH = 1
DEC_BATCH = 8
DEC_SEQ = 1
PAST_LEN = 1024
PAGE_SIZE = 128

N_HEADS_A = 8
HEAD_DIM_A = 64
MOBA_BLOCK = 256
MOBA_TOPK = 3
N_HEADS_B = 4
HEAD_DIM_B = 64
V_DIM_B = 2 * HEAD_DIM_B
WIDTH_A = N_HEADS_A * HEAD_DIM_A
WIDTH_B = N_HEADS_B * 2 * HEAD_DIM_B
D_IN = 3 * WIDTH_A + 3 * WIDTH_B + 2 * D_MODEL
D_FF = 2816
N_MOD = 9
Q_BLOCK = 128
RMS_EPS = 1e-6

kernel_name = "hybrid_moba_diffattn_macaron_step"

def rms_norm(x, g):
    xf = x.astype(jnp.float32)
    y = xf * lax.rsqrt(jnp.mean(xf * xf, axis=-1, keepdims=True) + RMS_EPS)
    return (y * g.astype(jnp.float32)).astype(x.dtype)

def swiglu(h, w_gate, w_up, w_down):
    return (jax.nn.silu(h @ w_gate) * (h @ w_up)) @ w_down

def alibi_slopes(n_heads):
    return jnp.asarray([2.0 ** (-8.0 * (i + 1) / n_heads) for i in range(n_heads)], dtype=jnp.float32)

def lambda_init(layer):
    return 0.8 - 0.6 * math.exp(-0.3 * layer)

def moba_select(q, q_pos, k_means):
    H, Q, _ = q.shape
    nb = k_means.shape[1]
    q_blk = q_pos // MOBA_BLOCK
    score = jnp.einsum("hqd,hnd->hqn", q, k_means, preferred_element_type=jnp.float32)
    fully_past = jnp.arange(nb, dtype=jnp.int32)[None, :] < q_blk[:, None]
    score = jnp.where(fully_past[None], score, -jnp.inf)
    n_top = min(MOBA_TOPK, nb)
    _, top = lax.top_k(score, n_top)
    top_valid = jnp.arange(n_top, dtype=jnp.int32)[None, :] < q_blk[:, None]
    idx = jnp.concatenate([top.astype(jnp.int32),
                           jnp.broadcast_to(q_blk[None, :, None], (H, Q, 1))], axis=-1)
    valid = jnp.concatenate([jnp.broadcast_to(top_valid[None], (H, Q, n_top)),
                             jnp.ones((H, Q, 1), dtype=bool)], axis=-1)
    return idx, valid

def moba_attend(q, q_pos, k_sel, v_sel, key_pos, valid, slopes):
    H, Q, J, BS = key_pos.shape
    s = jnp.einsum("hqd,hqjkd->hqjk", q, k_sel, preferred_element_type=jnp.float32) * (q.shape[-1] ** -0.5)
    dist = (q_pos[None, :, None, None] - key_pos).astype(jnp.float32)
    s = s - slopes[:, None, None, None] * dist
    mask = valid[..., None] & (key_pos <= q_pos[None, :, None, None])
    s = jnp.where(mask, s, -jnp.inf)
    p = jax.nn.softmax(s.reshape(H, Q, J * BS), axis=-1).reshape(H, Q, J, BS)
    out = jnp.einsum("hqjk,hqjkd->hqd", p, v_sel.astype(jnp.float32))
    return out.astype(q.dtype)

def moba_prompt(q, k, v):
    B, S, H, DH = q.shape
    nb = -(-S // MOBA_BLOCK)
    pad = nb * MOBA_BLOCK - S
    padw = ((0, 0), (0, pad), (0, 0), (0, 0))
    kb = jnp.pad(k, padw).reshape(B, nb, MOBA_BLOCK, H, DH).transpose(0, 3, 1, 2, 4)
    vb = jnp.pad(v, padw).reshape(B, nb, MOBA_BLOCK, H, DH).transpose(0, 3, 1, 2, 4)
    k_means = jnp.mean(kb.astype(jnp.float32), axis=3)
    qh = q.transpose(0, 2, 1, 3)
    n_chunks = S // Q_BLOCK
    heads = jnp.arange(H, dtype=jnp.int32)[:, None, None]
    slopes = alibi_slopes(H)

    def one_block(i):
        b = i // n_chunks
        start = (i % n_chunks) * Q_BLOCK
        qc = lax.dynamic_slice_in_dim(qh[b], start, Q_BLOCK, axis=1)
        pos = start + jnp.arange(Q_BLOCK, dtype=jnp.int32)
        idx, valid = moba_select(qc, pos, k_means[b])
        key_pos = idx[..., None] * MOBA_BLOCK + jnp.arange(MOBA_BLOCK, dtype=jnp.int32)
        return moba_attend(qc, pos, kb[b, heads, idx], vb[b, heads, idx], key_pos, valid, slopes)

    out = lax.map(one_block, jnp.arange(B * n_chunks, dtype=jnp.int32))
    return out.reshape(B, n_chunks, H, Q_BLOCK, DH).transpose(0, 1, 3, 2, 4).reshape(B, S, H, DH)

def moba_sample(q, k_new, v_new, k_pool, v_pool, layer, page_table):
    DB, T, H, DH = q.shape
    n_pages = page_table.shape[1]
    past = n_pages * PAGE_SIZE
    nb = -(-(past + T) // MOBA_BLOCK)
    pad = nb * MOBA_BLOCK - past - T
    heads = jnp.arange(H, dtype=jnp.int32)[:, None, None]
    slopes = alibi_slopes(H)
    pos = past + jnp.arange(T, dtype=jnp.int32)

    def one_seq(q_s, k_s, v_s, pt):
        k_past = k_pool[layer, pt].reshape(past, H, DH)
        k_full = jnp.concatenate([k_past, k_s.astype(k_past.dtype),
                                  jnp.zeros((pad, H, DH), k_past.dtype)], axis=0)
        kb = k_full.reshape(nb, MOBA_BLOCK, H, DH).transpose(2, 0, 1, 3)
        k_means = jnp.mean(kb.astype(jnp.float32), axis=2)
        qh = q_s.transpose(1, 0, 2)
        idx, valid = moba_select(qh, pos, k_means)
        key_pos = idx[..., None] * MOBA_BLOCK + jnp.arange(MOBA_BLOCK, dtype=jnp.int32)
        k_sel = kb[heads, idx]
        in_past = key_pos < past
        page = pt[jnp.clip(key_pos // PAGE_SIZE, 0, n_pages - 1)]
        head_b = jnp.broadcast_to(heads[..., None], key_pos.shape)
        v_past = v_pool[layer, page, key_pos % PAGE_SIZE, head_b]
        v_cur = v_s[jnp.clip(key_pos - past, 0, T - 1), head_b]
        v_sel = jnp.where(in_past[..., None], v_past, v_cur.astype(v_past.dtype))
        return moba_attend(qh, pos, k_sel, v_sel, key_pos, valid, slopes)

    out = jax.vmap(one_seq)(q, k_new, v_new, page_table)
    return out.transpose(0, 2, 1, 3).astype(q.dtype)

def diff_attend(q, q_pos, k, v, key_pos, lam, slopes):
    s = jnp.einsum("bhcqd,bhckd->bhcqk", q, k, preferred_element_type=jnp.float32) * (q.shape[-1] ** -0.5)
    dist = (q_pos[:, None] - key_pos[None, :]).astype(jnp.float32)
    s = s - slopes[None, :, None, None, None] * dist
    s = jnp.where(key_pos[None, :] <= q_pos[:, None], s, -jnp.inf)
    p = jax.nn.softmax(s, axis=-1)
    w = p[:, :, 0] - lam * p[:, :, 1]
    return jnp.einsum("bhqk,bhkd->bhqd", w, v.astype(jnp.float32)).astype(q.dtype)

def diff_prompt(q, k, v, lam):
    B, S, H = q.shape[:3]
    qh = q.transpose(0, 2, 3, 1, 4)
    kh = k.transpose(0, 2, 3, 1, 4)
    vh = v.transpose(0, 2, 1, 3)
    key_pos = jnp.arange(S, dtype=jnp.int32)
    slopes = alibi_slopes(H)
    n_chunks = S // Q_BLOCK

    def one_block(c):
        start = c * Q_BLOCK
        qc = lax.dynamic_slice_in_dim(qh, start, Q_BLOCK, axis=3)
        pos = start + jnp.arange(Q_BLOCK, dtype=jnp.int32)
        return diff_attend(qc, pos, kh, vh, key_pos, lam, slopes)

    out = lax.map(one_block, jnp.arange(n_chunks, dtype=jnp.int32))
    return out.transpose(1, 0, 3, 2, 4).reshape(B, S, H, V_DIM_B)

def diff_sample(q, k_new, v_new, k_pool, v_pool, layer, page_table, lam):
    DB, T, H = q.shape[:3]
    past = page_table.shape[1] * PAGE_SIZE
    k_past = k_pool[layer, page_table].reshape(DB, past, H, 2, HEAD_DIM_B)
    v_past = v_pool[layer, page_table].reshape(DB, past, H, V_DIM_B)
    k_all = jnp.concatenate([k_past, k_new.astype(k_past.dtype)], axis=1)
    v_all = jnp.concatenate([v_past, v_new.astype(v_past.dtype)], axis=1)
    pos = past + jnp.arange(T, dtype=jnp.int32)
    key_pos = jnp.arange(past + T, dtype=jnp.int32)
    out = diff_attend(q.transpose(0, 2, 3, 1, 4), pos, k_all.transpose(0, 2, 3, 1, 4),
                      v_all.transpose(0, 2, 1, 3), key_pos, lam, alibi_slopes(H))
    return out.transpose(0, 2, 1, 3).astype(q.dtype)

def prompt_attend(q_a, k_a, v_a, q_b, k_b, v_b, lam):
    return moba_prompt(q_a, k_a, v_a), diff_prompt(q_b, k_b, v_b, lam)

def sample_attend(q_a, k_a, v_a, q_b, k_b, v_b, lam, k_moba_pool, v_moba_pool,
                  k_diff_pool, v_diff_pool, page_table, layer):
    o_a = moba_sample(q_a, k_a, v_a, k_moba_pool, v_moba_pool, layer, page_table)
    o_b = diff_sample(q_b, k_b, v_b, k_diff_pool, v_diff_pool, layer, page_table, lam)
    return o_a, o_b

def decoder_layer(x, c, lp, lam_init, attend):
    B, T, _ = x.shape
    mod = (jax.nn.silu(c) @ lp["w_ada"] + lp["b_ada"]).reshape(B, 1, N_MOD, D_MODEL)
    sh1, sc1, g1, sh2, sc2, g2, sh3, sc3, g3 = [mod[:, :, i] for i in range(N_MOD)]
    h = rms_norm(x, lp["norm_ffn1"]) * (1.0 + sc1) + sh1
    x = x + 0.5 * g1 * swiglu(h, lp["ffn1_w_gate"], lp["ffn1_w_up"], lp["ffn1_w_down"])
    h = rms_norm(x, lp["norm_mix"]) * (1.0 + sc2) + sh2
    proj = h @ lp["w_in"]
    cuts = [WIDTH_A, 2 * WIDTH_A, 3 * WIDTH_A, 3 * WIDTH_A + WIDTH_B,
            3 * WIDTH_A + 2 * WIDTH_B, 3 * WIDTH_A + 3 * WIDTH_B, 3 * WIDTH_A + 3 * WIDTH_B + D_MODEL]
    q_a, k_a, v_a, q_b, k_b, v_b, g_a, g_b = jnp.split(proj, cuts, axis=-1)
    q_a = rms_norm(q_a.reshape(B, T, N_HEADS_A, HEAD_DIM_A), lp["qn_moba"])
    k_a = rms_norm(k_a.reshape(B, T, N_HEADS_A, HEAD_DIM_A), lp["kn_moba"])
    v_a = v_a.reshape(B, T, N_HEADS_A, HEAD_DIM_A)
    q_b = rms_norm(q_b.reshape(B, T, N_HEADS_B, 2, HEAD_DIM_B), lp["qn_diff"])
    k_b = rms_norm(k_b.reshape(B, T, N_HEADS_B, 2, HEAD_DIM_B), lp["kn_diff"])
    v_b = v_b.reshape(B, T, N_HEADS_B, V_DIM_B)
    lam = (jnp.exp(jnp.sum(lp["lambda_q1"].astype(jnp.float32) * lp["lambda_k1"].astype(jnp.float32)))
           - jnp.exp(jnp.sum(lp["lambda_q2"].astype(jnp.float32) * lp["lambda_k2"].astype(jnp.float32)))
           + lam_init)
    o_a, o_b = attend(q_a, k_a, v_a, q_b, k_b, v_b, lam)
    o_b = rms_norm(o_b, lp["subln_diff"]) * (1.0 - lam_init)
    y_a = o_a.reshape(B, T, WIDTH_A) @ lp["w_branch_moba"]
    y_b = o_b.reshape(B, T, WIDTH_B) @ lp["w_branch_diff"]
    mixed = (jax.nn.sigmoid(g_a) * y_a + jax.nn.sigmoid(g_b) * y_b) @ lp["w_out"]
    x = x + g2 * mixed
    h = rms_norm(x, lp["norm_ffn2"]) * (1.0 + sc3) + sh3
    x = x + 0.5 * g3 * swiglu(h, lp["ffn2_w_gate"], lp["ffn2_w_up"], lp["ffn2_w_down"])
    rows = (k_a, v_a, k_b.reshape(B, T, N_HEADS_B, 2 * HEAD_DIM_B), v_b)
    return x, rows

def setup_inputs(seed: int = 0) -> dict:
    key = jax.random.key(seed)
    ks = iter(jax.random.split(key, 48))
    f32 = jnp.float32
    n_pages = PAST_LEN // PAGE_SIZE
    n_used = DEC_BATCH * n_pages
    n_phys = n_used + max(1, n_used // 4)

    def nrm(shape, scale=1.0):
        return jax.random.normal(next(ks), shape, f32) * scale

    def gain(shape):
        return 1.0 + 0.02 * nrm(shape)

    page_table = jax.random.permutation(next(ks), n_phys)[:n_used].reshape(DEC_BATCH, n_pages).astype(jnp.int32)
    return {
        "x_prompt": nrm((BATCH, SEQ, D_MODEL)),
        "x_sample": nrm((DEC_BATCH, DEC_SEQ, D_MODEL)),
        "cache_k_moba": nrm((DEPTH, n_phys, PAGE_SIZE, N_HEADS_A, HEAD_DIM_A)),
        "cache_v_moba": nrm((DEPTH, n_phys, PAGE_SIZE, N_HEADS_A, HEAD_DIM_A)),
        "cache_k_diff": nrm((DEPTH, n_phys, PAGE_SIZE, N_HEADS_B, 2 * HEAD_DIM_B)),
        "cache_v_diff": nrm((DEPTH, n_phys, PAGE_SIZE, N_HEADS_B, V_DIM_B)),
        "page_table": page_table,
        "c_prompt": nrm((BATCH, D_MODEL)),
        "c_sample": nrm((DEC_BATCH, D_MODEL)),
        "w_ada": nrm((DEPTH, D_MODEL, N_MOD * D_MODEL), 0.5 * D_MODEL ** -0.5),
        "b_ada": nrm((DEPTH, N_MOD * D_MODEL), 0.02),
        "norm_ffn1": gain((DEPTH, D_MODEL)),
        "ffn1_w_gate": nrm((DEPTH, D_MODEL, D_FF), D_MODEL ** -0.5),
        "ffn1_w_up": nrm((DEPTH, D_MODEL, D_FF), D_MODEL ** -0.5),
        "ffn1_w_down": nrm((DEPTH, D_FF, D_MODEL), D_FF ** -0.5),
        "norm_mix": gain((DEPTH, D_MODEL)),
        "w_in": nrm((DEPTH, D_MODEL, D_IN), D_MODEL ** -0.5),
        "qn_moba": gain((DEPTH, HEAD_DIM_A)),
        "kn_moba": gain((DEPTH, HEAD_DIM_A)),
        "qn_diff": gain((DEPTH, HEAD_DIM_B)),
        "kn_diff": gain((DEPTH, HEAD_DIM_B)),
        "lambda_q1": nrm((DEPTH, HEAD_DIM_B), 0.1),
        "lambda_k1": nrm((DEPTH, HEAD_DIM_B), 0.1),
        "lambda_q2": nrm((DEPTH, HEAD_DIM_B), 0.1),
        "lambda_k2": nrm((DEPTH, HEAD_DIM_B), 0.1),
        "subln_diff": gain((DEPTH, V_DIM_B)),
        "w_branch_moba": nrm((DEPTH, WIDTH_A, D_MODEL), WIDTH_A ** -0.5),
        "w_branch_diff": nrm((DEPTH, WIDTH_B, D_MODEL), WIDTH_B ** -0.5),
        "w_out": nrm((DEPTH, D_MODEL, D_MODEL), D_MODEL ** -0.5),
        "norm_ffn2": gain((DEPTH, D_MODEL)),
        "ffn2_w_gate": nrm((DEPTH, D_MODEL, D_FF), D_MODEL ** -0.5),
        "ffn2_w_up": nrm((DEPTH, D_MODEL, D_FF), D_MODEL ** -0.5),
        "ffn2_w_down": nrm((DEPTH, D_FF, D_MODEL), D_FF ** -0.5),
    }

def reference(x_prompt, x_sample, cache_k_moba, cache_v_moba, cache_k_diff, cache_v_diff, page_table,
              c_prompt, c_sample, w_ada, b_ada, norm_ffn1, ffn1_w_gate, ffn1_w_up, ffn1_w_down,
              norm_mix, w_in, qn_moba, kn_moba, qn_diff, kn_diff, lambda_q1, lambda_k1, lambda_q2,
              lambda_k2, subln_diff, w_branch_moba, w_branch_diff, w_out, norm_ffn2, ffn2_w_gate,
              ffn2_w_up, ffn2_w_down):
    y_prompt, y_sample = x_prompt, x_sample
    rows_prompt, rows_sample = [], []
    for l in range(DEPTH):
        lp = {
            "w_ada": w_ada[l], "b_ada": b_ada[l],
            "norm_ffn1": norm_ffn1[l], "ffn1_w_gate": ffn1_w_gate[l], "ffn1_w_up": ffn1_w_up[l],
            "ffn1_w_down": ffn1_w_down[l], "norm_mix": norm_mix[l], "w_in": w_in[l],
            "qn_moba": qn_moba[l], "kn_moba": kn_moba[l], "qn_diff": qn_diff[l], "kn_diff": kn_diff[l],
            "lambda_q1": lambda_q1[l], "lambda_k1": lambda_k1[l], "lambda_q2": lambda_q2[l],
            "lambda_k2": lambda_k2[l], "subln_diff": subln_diff[l],
            "w_branch_moba": w_branch_moba[l], "w_branch_diff": w_branch_diff[l], "w_out": w_out[l],
            "norm_ffn2": norm_ffn2[l], "ffn2_w_gate": ffn2_w_gate[l], "ffn2_w_up": ffn2_w_up[l],
            "ffn2_w_down": ffn2_w_down[l],
        }
        lam_init = lambda_init(l)
        y_prompt, r_p = decoder_layer(y_prompt, c_prompt, lp, lam_init, prompt_attend)
        attend_s = functools.partial(sample_attend, k_moba_pool=cache_k_moba, v_moba_pool=cache_v_moba,
                                     k_diff_pool=cache_k_diff, v_diff_pool=cache_v_diff,
                                     page_table=page_table, layer=l)
        y_sample, r_s = decoder_layer(y_sample, c_sample, lp, lam_init, attend_s)
        rows_prompt.append(r_p)
        rows_sample.append(r_s)
    k_moba_prompt = jnp.stack([r[0] for r in rows_prompt])
    v_moba_prompt = jnp.stack([r[1] for r in rows_prompt])
    k_diff_prompt = jnp.stack([r[2] for r in rows_prompt])
    v_diff_prompt = jnp.stack([r[3] for r in rows_prompt])
    k_moba_sample = jnp.stack([r[0] for r in rows_sample])
    v_moba_sample = jnp.stack([r[1] for r in rows_sample])
    k_diff_sample = jnp.stack([r[2] for r in rows_sample])
    v_diff_sample = jnp.stack([r[3] for r in rows_sample])
    return (y_prompt, y_sample, k_moba_prompt, v_moba_prompt, k_diff_prompt, v_diff_prompt,
            k_moba_sample, v_moba_sample, k_diff_sample, v_diff_sample)


_drawn_inputs = setup_inputs


def setup_inputs(seed=0):
    import zlib

    import numpy as np

    out = dict(_drawn_inputs(seed))
    spreads = {}
    factors = {'norm_ffn1': 8.0,
     'norm_mix': 2.861,
     'qn_moba': 64.0,
     'kn_moba': 8.058,
     'qn_diff': 25.713,
     'kn_diff': 8.621,
     'lambda_q1': 8.0,
     'lambda_k1': 8.0,
     'lambda_q2': 4.705,
     'lambda_k2': 3.129,
     'subln_diff': 64.0,
     'norm_ffn2': 21.955,
     'cache_v_moba': 2.727}
    for name, (base, spread) in spreads.items():
        noise = np.random.default_rng([zlib.crc32(name.encode()), seed]).standard_normal(out[name].shape)
        drawn = base * np.exp(spread * noise) if base else spread * noise
        out[name] = __import__('jax').numpy.asarray(drawn.astype(out[name].dtype))
    for name, factor in factors.items():
        out[name] = (out[name] * factor).astype(out[name].dtype)
    return out
```

```python
from contextlib import ExitStack

import numpy as np
import concourse.bass as bass
from concourse import mybir

F32 = mybir.dt.float32
F32R = mybir.dt.float32r
I32 = mybir.dt.int32
ALU = mybir.AluOpType
ACT = mybir.ActivationFunctionType
AX = mybir.AxisListType

P = 128
D = 1024
KC = D // P
TP = 256
TS = 8
T = TP + TS
FF = 2816
FC = FF // P
NPAIR = FC // 2
NMOD = 9
PAST = 1024
PAGE = 128
NPG = PAST // PAGE
NPHYS = 80
EPS = 1e-6
LAM_INIT = 0.2
UNIT = 2048
SLOTS = 4
ADAC = NMOD * D // 512
RW = 152
BIG = 1e30

W_FF1, W_DN1 = 0, 22
W_QKV, W_GATE, W_BR, W_OUT = 34, 46, 54, 58
W_FF2, W_DN2 = 62, 84
ADA_PRO = 4


def stream_plan():
    plan = []
    ada = lambda c: [("ada", c, 0), ("ada", c, 1)]
    for c in range(ADA_PRO):
        plan += ada(c)
    for i in range(NPAIR):
        plan += [("w", W_FF1 + 2 * i)] + ada(ADA_PRO + i) + [("w", W_FF1 + 2 * i + 1)]
    for i in range(2):
        plan += [("w", W_DN1 + 6 * i + u) for u in range(6)] + ada(ADA_PRO + NPAIR + i)
    plan += [("w", W_QKV + u) for u in range(6)] + ada(ADAC - 1)
    plan += [("w", n) for n in range(W_QKV + 6, W_DN2 + 12)]
    return plan


PLAN = stream_plan()
POS = {key: i for i, key in enumerate(PLAN)}


def slot_of(key):
    return POS[key] % SLOTS


def landed(key):
    return 16 * (POS[key] // SLOTS + 1)


CW = {}


def _columns():
    at = 0
    for name, w in (("ident", 128), ("blockdiag", 128), ("ones", 128), ("half", 2), ("sel9", 9), ("sel8", 8),
                    ("negslope", 1), ("pageslope", 8), ("coef1", 1), ("coeflam", 1), ("rowA", 1), ("tri", 16),
                    ("dist", 384), ("distrow", 128), ("maskA", 512), ("maskB", 512)):
        CW[name] = (at, w)
        at += w
    return at


NCONST = _columns()


def slope_of_row(j):
    return 2.0 ** -(j + 1) if j < 8 else 2.0 ** (-2.0 * ((j - 8) // 2 + 1))


def constants():
    c = np.zeros((P, NCONST), np.float32)

    def put(name, a):
        c[:, CW[name][0]:CW[name][0] + CW[name][1]] = a

    p = np.arange(P)
    put("ident", np.eye(P))
    put("blockdiag", p[:, None] // 64 == p[None] // 64)
    put("ones", 1.0)
    put("half", np.stack([p < 64, p >= 64], 1))
    put("sel9", (p[:, None] % 32) == np.arange(9)[None])
    put("sel8", (p[:, None] // 16) == np.arange(8)[None])
    slope = np.array([slope_of_row(r % 16) for r in p])
    put("negslope", -slope[:, None])
    put("pageslope", slope[:, None] * 128.0 * np.arange(8)[None])
    isb1 = ((p % 16) >= 8) & (p % 2 == 1)
    put("coef1", (~isb1)[:, None])
    put("coeflam", isb1[:, None])
    put("rowA", ((p % 16) < 8)[:, None])
    n = np.arange(4)
    put("tri", np.broadcast_to((n[None, :] < n[:, None]).reshape(1, 16), (P, 16)))
    k = np.arange(256)
    d0 = np.where(k[None, :128] <= p[:, None], p[:, None] - k[None, :128], BIG)
    d1 = np.where(k[None] <= p[:, None] + 128, p[:, None] + 128 - k[None], BIG)
    put("dist", np.concatenate([d0, d1], 1))
    put("distrow", np.broadcast_to(PAST - np.arange(128)[None], (P, 128)))
    m = p % 32
    col = np.arange(512)
    put("maskA", (col[None] // 64 == m[:, None]))
    put("maskB", (m[:, None] < 8) & (col[None] // 128 == m[:, None] // 2))
    return c


R_BADA, R_N1, R_N2, R_N3, R_QNA, R_KNA, R_QNB, R_KNB, R_SUB, R_LQ, R_LK, NROWS = 0, 72, 80, 88, 96, 97, 98, 99, 100, 101, 102, 103


class Chain:

    def __init__(self, eng, sem):
        self.eng, self.sem, self.base, self.n = eng, sem, 0, 0

    def link(self, ins):
        ins.then_inc(self.sem, 1)
        self.n += 1
        self.eng.wait_ge(self.sem, self.base + self.n)

    def enter(self, i, first, per):
        self.base, self.n, self.per = self.n + (i - first) * per, 0, per
        self.at = self.base

    def leave(self, before, count):
        assert self.n == self.per
        self.base, self.n = 0, before + count * self.per


def build(nc, A, O):
    ctx = ExitStack()
    with ctx:
        at = [((nc.sbuf_base + 31) // 32) * 32]
        end = nc.sbuf_usable_end

        def place(name, shape, dt=F32, where=None):
            size = int(np.prod(shape[1:])) * 4
            where = where if where is not None else at
            h = nc.alloc_sbuf_tensor_at(name, shape, dt, offset=where[0])
            where[0] = (where[0] + size + 31) // 32 * 32
            assert where[0] <= end, (name, where[0], end)
            return h

        def sem(name):
            return ctx.enter_context(nc.semaphore(name))

        const = place("const", [P, NCONST])
        raw = [place(f"raw{s}", [P, UNIT]) for s in range(SLOTS)]
        whi = [place(f"whi{s}", [P, UNIT], F32R) for s in range(2)]
        wlo = [place(f"wlo{s}", [P, UNIT], F32R) for s in range(2)]
        x = place("x", [P, KC, T])
        hhi = place("hhi", [P, KC, T], F32R)
        hlo = place("hlo", [P, KC, T], F32R)
        mod = place("mod", [P, NMOD * KC, 9])
        par = place("par", [P, NROWS])
        adarow = place("adarow", [P, 512])
        csilu = place("csilu", [P, KC, 32])
        work = place("work", [P, KC, T])
        rstd = place("rstd", [P, 2, T])
        misc = place("misc", [P, 64])
        tmps = place("tmps", [P, 2, TS])
        region = at[0]
        r = [region]
        ahi = place("ahi", [P, FC, T], F32R, r)
        alo = place("alo", [P, FC, T], F32R, r)
        sil = place("sil", [P, 2, T], where=r)
        act = place("act", [P, 2, T], where=r)
        yst = place("yst", [P, 2, D], where=r)
        ysts = place("ysts", [TS, D], where=r)
        r = [region]
        xtok = place("xtok", [P, 2, D], where=r)
        xtoks = place("xtoks", [TS, D], where=r)
        rows = place("rows", [NROWS, P], where=r)
        crow = place("crow", [72, P], where=r)
        r = [region]
        kv = [[place(f"kv{a}{s}", [P, 4, 512], where=r) for s in range(2)] for a in "AB"]
        qT = place("qT", [P, KC, T], where=r)
        kT = place("kT", [P, KC, T], where=r)
        vtok = place("vtok", [P, 2, D], where=r)
        vtoks = place("vtoks", [TS, D], where=r)
        gT = place("gT", [P, 2 * KC, T], where=r)
        stat = place("stat", [P, 64], where=r)
        sall = place("sall", [P, NPG, RW], where=r)
        area = r[0]
        r = [area]
        vT = place("vT", [P, 2, T], where=r)
        kst = place("kst", [P, 2, 256], where=r)
        ksts = place("ksts", [TS, 256], where=r)
        sqb = place("sqb", [P, 2, T], where=r)
        r = [area]
        qb = [place(f"qb{s}", [P, D], where=r) for s in range(2)]
        r = [area]
        prob = place("prob", [P, PAST], where=r)
        b0 = place("b0", [P, P], where=r)
        ecur = place("ecur", [P, P], where=r)
        dcur = place("dcur", [TS, RW], where=r)
        r = [area]
        plog = [place(f"plog{h}", [P, 384], where=r) for h in range(2)]
        assert r[0] <= area + 4096
        r[0] = area + 4096 + 1024 + 640
        om = place("om", [P, 2, 512], where=r)
        pts = [place(f"pts{h}", [P, 384], where=r) for h in range(2)]
        r = [area]
        osq = place("osq", [P, 4, T], where=r)
        prodc = ecur

        bank = ctx.enter_context(nc.psum_tensor("bank", [P, 8, 512], F32))

        def C(name, lo=0, hi=None):
            a, w = CW[name]
            return const[:, a + lo:a + (w if hi is None else hi)]

        ident = C("ident")

        s_raw = [sem(f"raw_landed{s}") for s in range(SLOTS)]
        s_rows, s_crow, s_x, s_const = sem("rows_landed"), sem("crow_landed"), sem("x_landed"), sem("const_landed")
        s_hi, s_lo, s_gemm = sem("hi_ready"), sem("lo_ready"), sem("gemm_done")
        s_ada, s_adarow, s_sel, s_mod = sem("ada_multiplied"), sem("adarow_ready"), sem("ada_turned"), sem("mod_ready")
        s_zero = sem("csilu_zeroed")
        s_parT, s_par, s_csilu = sem("params_turned"), sem("params_ready"), sem("csilu_ready")
        s_xT, s_xfirst = sem("x_turned"), sem("x_first")
        s_sq, s_ssum, s_var, s_rstd = sem("squares_ready"), sem("squares_summed"), sem("variance_ready"), sem("rstd_ready")
        s_h, s_hhi, s_hlo = sem("h_ready"), sem("hhi_ready"), sem("hlo_ready")
        s_sil, s_act, s_ahi, s_alo = sem("silu_ready"), sem("act_ready"), sem("ahi_ready"), sem("alo_ready")
        s_xup = sem("x_updated")
        s_coef = sem("coefficients_ready")
        s_lamsum, s_lamexp = sem("lambda_sums"), sem("lambda_exp")
        s_proj, s_nsum, s_nvar, s_nrstd, s_qk = sem("proj_out"), sem("head_squares_summed"), sem("head_variance"), sem("head_rstd"), sem("qk_ready")
        s_turn, s_tok, s_rowout = sem("kv_turned"), sem("kv_tokens_ready"), sem("kv_rows_stored")
        s_qbp, s_qb = sem("q_spread"), sem("q_spread_ready")
        s_kv = [[sem(f"kv_landed{a}{s}") for s in range(2)] for a in "AB"]
        s_mul, s_red = sem("kq_multiplied"), sem("scores_ready")
        s_gexp, s_sig = sem("gate_exp"), sem("gate_ready")
        s_ecur, s_cur = sem("current_products"), sem("current_scores")
        s_lT, s_logit, s_prob, s_pscaled, s_diag = sem("scores_turned"), sem("logits_ready"), sem("probs_ready"), sem("probs_scaled"), sem("diag_ready")
        s_dps, s_dcur = sem("current_weights_psum"), sem("current_weights_ready")
        s_pT, s_pTs = sem("probs_turned"), sem("probs_turned_ready")
        s_pv, s_pvd, s_om, s_ext = sem("v_used"), sem("sample_out"), sem("sample_masked"), sem("sample_extracted")
        s_psc, s_plog, s_pexp, s_pscale = sem("prompt_scores"), sem("prompt_logits"), sem("prompt_exp"), sem("prompt_probs")
        s_ppT, s_pps, s_po, s_pout = sem("prompt_probs_turned"), sem("prompt_probs_ready"), sem("prompt_out"), sem("prompt_out_ready")
        s_samp = sem("sample_out_ready")
        s_osq, s_osum, s_ovar, s_orstd, s_o = sem("o_squares"), sem("o_summed"), sem("o_variance"), sem("o_rstd"), sem("o_ready")
        s_mix = sem("mix_ready")
        s_yT, s_ys, s_yout = sem("y_turned"), sem("y_staged"), sem("y_stored")
        s_vch, s_ach = sem("vector_steps"), sem("scalar_steps")

        block = ctx.enter_context(nc.Block())

        gate_w = (A["ffn1_w_gate"], A["ffn2_w_gate"])
        up_w = (A["ffn1_w_up"], A["ffn2_w_up"])
        down_w = (A["ffn1_w_down"], A["ffn2_w_down"])

        def km(w):
            return w[0].rearrange("(k p) n -> p k n", p=P)

        def ff_block(w, i):
            return km(w)[:, :, bass.ds(i * 256, 256)]

        def fixed_block(n):
            for first, w in ((W_DN1, down_w[0]), (W_DN2, down_w[1])):
                if first <= n < first + 12:
                    cb, third = divmod(n - first, 3)
                    k1 = min(FC, 8 * third + 8)
                    return km(w)[:, 8 * third:k1, cb * 256:cb * 256 + 256], k1 - 8 * third, 256
            if W_QKV <= n < W_BR:
                c = (n - W_QKV) * 256
                return km(A["w_in"])[:, :, c:c + 256], KC, 256
            if W_BR <= n < W_OUT:
                w = A["w_branch_diff"] if (n - W_BR) % 2 else A["w_branch_moba"]
                c = (n - W_BR) // 2 * 512
                return km(w)[:, :, c:c + 512], 4, 512
            c = (n - W_OUT) * 256
            return km(A["w_out"])[:, :, c:c + 256], KC, 256

        def width_of(n):
            if W_FF1 <= n < W_DN1 or W_FF2 <= n < W_DN2:
                return UNIT
            _, nk, w = fixed_block(n)
            return nk * w

        CACHE_K = (A["cache_k_moba"][0].rearrange("n t h d -> n t (h d)"), A["cache_k_diff"][0].rearrange("n t h d -> n t (h d)"))
        CACHE_V = (A["cache_v_moba"][0].rearrange("n t h d -> n t (h d)"), A["cache_v_diff"][0].rearrange("n t h d -> n t (h d)"))

        def load_half(eng, ab, cache, s, half, use):
            for q in range(4):
                g = 4 * half + q
                page = eng.value_load(A["page_table"][s:s + 1, g:g + 1], min_val=0, max_val=NPHYS - 1)
                eng.dma_start(kv[ab][use % 2][:, q, :], cache[bass.ds(page, 1)].rearrange("a t d -> (a t) d")).then_inc(s_kv[ab][use % 2], 16)

        def kv_landed(use):
            return 64 * (use // 2 + 1)

        def kv_load(eng, ab, use):
            s, half = divmod(use % 16, 2)
            if use >= 2:
                prev = use - 2
                ps, ph = divmod(prev % 16, 2)
                eng.wait_ge(s_red if prev < 16 else s_pv, 4 * ps + 2 * ph + ab + 1)
            load_half(eng, ab, (CACHE_K if use < 16 else CACHE_V)[ab], s, half, use)

        @block.sync
        def _(sp):
            sp.dma_start(rows[:, :], A["params"]).then_inc(s_rows, 16)
            sp.dma_start(crow[:, :], A["c_rows"]).then_inc(s_crow, 16)
            sp.dma_start(const[:, :], A["consts"]).then_inc(s_const, 16)
            sp.dma_start(xtok[:, :, :], A["x_prompt"][0].rearrange("(a p) d -> p a d", p=P)).then_inc(s_x, 16)
            sp.dma_start(xtoks[:, :], A["x_sample"][:, 0, :]).then_inc(s_x, 16)

            def slot_free(key, shift=0):
                if POS[key] < SLOTS:
                    return
                prev = PLAN[POS[key] - SLOTS]
                if prev[0] == "ada":
                    sp.wait_ge(s_ada, prev[1] + 1 + shift)
                else:
                    sp.wait_ge(s_lo, prev[1] + 1 + shift)

            def load_ada(c, half, key, shift=0):
                slot_free(key, shift)
                src = A["w_ada"][0].rearrange("(k p) n -> p k n", p=P)[:, 4 * half:4 * half + 4, bass.ds(c * 512, 512)]
                s = slot_of(key)
                sp.dma_start(raw[s][:, :].rearrange("p (k n) -> p k n", k=4), src).then_inc(s_raw[s], 16)

            def load_w(n):
                src, nk, w = fixed_block(n)
                slot_free(("w", n))
                s = slot_of(("w", n))
                sp.dma_start(raw[s][:, 0:nk * w].rearrange("p (k n) -> p k n", k=nk), src).then_inc(s_raw[s], 16)

            def load_ff(w, i, key, shift=0):
                slot_free(key, shift)
                s = slot_of(key)
                sp.dma_start(raw[s][:, :].rearrange("p (k n) -> p k n", k=KC), ff_block(w, i)).then_inc(s_raw[s], 16)

            for c in range(ADA_PRO):
                for half in range(2):
                    load_ada(c, half, ("ada", c, half))

            def ff1_step(i, first, rate):
                d = i - first if rate else 0
                load_ff(gate_w[0], i, ("w", W_FF1 + 2 * first), 2 * d)
                load_ada(ADA_PRO + i, 0, ("ada", ADA_PRO + first, 0), d)
                load_ada(ADA_PRO + i, 1, ("ada", ADA_PRO + first, 1), d)
                load_ff(up_w[0], i, ("w", W_FF1 + 2 * first + 1), 2 * d)

            ff1_step(0, 0, 0)
            with sp.Fori(1, NPAIR) as i:
                ff1_step(i, 1, 1)
            for i in range(2):
                for u in range(6):
                    load_w(W_DN1 + 6 * i + u)
                c = ADA_PRO + NPAIR + i
                for half in range(2):
                    load_ada(c, half, ("ada", c, half))
            for u in range(6):
                load_w(W_QKV + u)
            for half in range(2):
                load_ada(ADAC - 1, half, ("ada", ADAC - 1, half))
            sp.wait_ge(s_gemm, W_QKV)
            kv_load(sp, 0, 0)
            kv_load(sp, 0, 1)
            for u in range(6, 12):
                load_w(W_QKV + u)
            for n in range(W_GATE, W_GATE + 3):
                load_w(n)
            for s in range(TS):
                load_w(W_GATE + 3 + s)
                for half in range(2):
                    kv_load(sp, 0, 2 * (s + 1) + half)
            for n in range(W_BR + 3, W_BR + 6):
                load_w(n)
            for s in range(TS - 1):
                for half in range(2):
                    kv_load(sp, 0, 16 + 2 * (s + 1) + half)
            for n in range(W_BR + 6, W_FF2):
                load_w(n)

            def ff2_pair(i, key_pair, d):
                load_ff(gate_w[1], i, ("w", W_FF2 + 2 * key_pair), 2 * d)
                load_ff(up_w[1], i, ("w", W_FF2 + 2 * key_pair + 1), 2 * d)

            ff2_pair(0, 0, 0)
            ff2_pair(1, 1, 0)
            with sp.Fori(1, NPAIR // 2) as i:
                ff2_pair(2 * i, 2, 2 * (i - 1))
                ff2_pair(2 * i + 1, 3, 2 * (i - 1))
            ff2_pair(NPAIR - 1, NPAIR - 1, 0)
            for u in range(12):
                load_w(W_DN2 + u)
            for cb in range(4):
                sp.wait_ge(s_ys, 2 * (cb + 1))
                sp.dma_start(O["y_prompt"][0].rearrange("(a p) d -> p a d", p=P)[:, :, cb * 256:cb * 256 + 256],
                             yst[:, :, cb * 256:cb * 256 + 256]).then_inc(s_yout, 16)
                sp.dma_start(O["y_sample"][:, 0, cb * 256:cb * 256 + 256], ysts[:, cb * 256:cb * 256 + 256]).then_inc(s_yout, 16)
            sp.wait_ge(s_yout, 16 * 8)
            sp.wait_ge(s_rowout, 16 * 16)

        @block.gpsimd
        def _(pool):
            turned = 0
            for u in range(12):
                ab, kind, p = u // 6, u % 6 // 2, u % 2
                if kind == 0:
                    continue
                turned += 1
                pool.wait_ge(s_tok, 2 * turned)
                c0 = 256 * p
                name = ("k", "v")[kind - 1] + ("_moba", "_diff")[ab]
                dst = O[name + "_prompt"][0, 0].rearrange("(a p) h d -> p a (h d)", p=P)[:, :, c0:c0 + 256]
                dsts = O[name + "_sample"][0, :, 0].rearrange("s h d -> s (h d)")[:, c0:c0 + 256]
                f0 = 512 * ab + c0
                src = kst[:, :, :] if kind == 1 else vtok[:, :, f0:f0 + 256]
                srcs = ksts[:, :] if kind == 1 else vtoks[:, f0:f0 + 256]
                pool.dma_start(dst, src).then_inc(s_rowout, 16)
                pool.dma_start(dsts, srcs).then_inc(s_rowout, 16)
            for s in range(TS):
                pool.wait_ge(s_qb, s + 1)
                for half in range(2):
                    for ab in range(2):
                        use = 2 * s + half
                        pool.wait_ge(s_kv[ab][use % 2], kv_landed(use))
                        k = kv[ab][use % 2][:, :, :]
                        qrow = qb[s % 2][:, 512 * ab:512 * ab + 512].unsqueeze(1).broadcast_to([P, 4, 512])
                        nc.gpsimd.tensor_tensor(k, k, qrow, ALU.mult).then_inc(s_mul, 1)

        @block.scalar
        def _(a):
            ch = Chain(a, s_ach)

            def hi(n, key=None, d=0, ext=0):
                key = key or ("w", n)
                s = slot_of(key)
                a.wait_ge(s_raw[s], landed(key) + 16 * d)
                if not (isinstance(n, int) and n < 2):
                    a.wait_ge(s_gemm, n - 1)
                w = UNIT if ext == 0 else ext
                nc.scalar.activation(whi[key[1] % 2][:, 0:w], raw[s][:, 0:w], ACT.Copy).then_inc(s_hi, 1)

            def ada_row(c):
                a.wait_ge(s_ada, c + 1)
                if not (isinstance(c, int) and c == 0):
                    a.wait_ge(s_sel, c)
                nc.scalar.activation(adarow[:, :], bank[:, 4, :], ACT.Copy).then_inc(s_adarow, 1)

            def norm(t):
                a.wait_ge(*((s_xfirst, 2) if t == 0 else (s_xup, (4, 8)[t - 1])))
                nc.scalar.activation(work[:, :, :], x[:, :, :], ACT.Square).then_inc(s_sq, 1)
                a.wait_ge(s_var, t + 1)
                nc.scalar.activation(rstd[:, 0, :], rstd[:, 0, :], ACT.Sqrt).then_inc(s_rstd, 1)
                for half in range(2):
                    a.wait_ge(s_h, 2 * t + half + 1)
                    nc.scalar.activation(hhi[:, 4 * half:4 * half + 4, :], work[:, 4 * half:4 * half + 4, :], ACT.Copy).then_inc(s_hhi, 1)

            def silu(i):
                a.wait_ge(s_gemm, silu.base + 2 * i + 1)
                if not (isinstance(i, int) and i == 0 and silu.pairs == 0):
                    a.wait_ge(s_act, silu.pairs + i)
                nc.scalar.activation(sil[:, :, :], bank[:, 0:2, 0:T], ACT.Silu).then_inc(s_sil, 1)

            def act_hi(i):
                a.wait_ge(s_act, silu.pairs + i + 1)
                nc.scalar.activation(ahi[:, bass.ds(2 * i, 2), :], act[:, :, :], ACT.Copy).then_inc(s_ahi, 1)

            a.wait_ge(s_parT, 1)
            a.wait_ge(s_zero, 1)
            nc.scalar.activation(csilu[:, :, 0:9], bank[:, 6, 0:72].rearrange("p (k m) -> p k m", k=KC), ACT.Silu).then_inc(s_csilu, 1)
            a.wait_ge(s_lamsum, 1)
            nc.scalar.activation(misc[:, 4:6], bank[:, 6, 0:2], ACT.Exp).then_inc(s_lamexp, 1)
            for c in range(ADA_PRO):
                ada_row(c)
            hi(W_FF1)
            norm(0)
            silu.base, silu.pairs = W_FF1, 0

            def ff1_turn(i, key_i, d):
                hi(W_FF1 + 2 * i + 1, ("w", W_FF1 + 2 * key_i + 1), d)
                silu(i)
                ada_row(ADA_PRO + i)
                hi(W_FF1 + 2 * i + 2, ("w", W_FF1 + 2 * key_i + 2), d)
                act_hi(i)

            ff1_turn(0, 0, 0)
            with a.Fori(1, NPAIR) as i:
                ff1_turn(i, 1, i - 1)

            def down(first, ada):
                for u in range(12):
                    n = first + u
                    if u:
                        hi(n, ext=width_of(n))
                    if ada and u in (6, 11):
                        ada_row(ADA_PRO + NPAIR + (u == 11))

            down(W_DN1, True)
            hi(W_QKV)
            a.wait_ge(s_gemm, W_QKV)
            kv_load(a, 1, 0)
            kv_load(a, 1, 1)
            norm(1)

            nsq = 0
            toks = 0

            def head_rstd(k):
                a.wait_ge(s_nvar, k)
                nc.scalar.activation(rstd[:, :, :], rstd[:, :, :], ACT.Sqrt).then_inc(s_nrstd, 1)

            for u in range(12):
                n = W_QKV + u
                ab, kind, p = u // 6, u % 6 // 2, u % 2
                hi(n + 1)
                if u > 0 and (u - 1) % 6 // 2 < 2:
                    head_rstd(nsq)
                b = 2 * (u % 2)
                c0 = 4 * ab + 2 * p
                a.wait_ge(s_gemm, n + 1)
                src = bank[:, b:b + 2, 0:T]
                if kind < 2:
                    dst = (qT, kT)[kind]
                    nc.scalar.activation(dst[:, c0:c0 + 2, :], src, ACT.Copy)
                    if nsq:
                        a.wait_ge(s_nsum, nsq)
                    nc.scalar.activation(sqb[:, :, :], src, ACT.Square).then_inc(s_proj, 1)
                    nsq += 1
                else:
                    if toks:
                        a.wait_ge(s_turn, toks)
                    nc.scalar.activation(vT[:, :, :], src, ACT.Copy).then_inc(s_proj, 1)
                if kind > 0:
                    toks += 1
                if u == 6:
                    ada_row(ADAC - 1)
            for s in range(TS):
                a.wait_ge(s_qbp, s + 1)
                if s == 0:
                    a.wait_ge(s_rowout, 16 * 16)
                    a.wait_ge(s_turn, 8)
                if s >= 2:
                    a.wait_ge(s_mul, 4 * (s - 1))
                b = 4 + 2 * (s % 2)
                nc.scalar.activation(qb[s % 2][:, :].rearrange("p (a n) -> p a n", a=2), bank[:, b:b + 2, :], ACT.Copy).then_inc(s_qb, 1)
                hi(W_GATE + s + 1, ext=width_of(W_GATE + s + 1))
                if s + 1 < TS:
                    kv_load(a, 1, 2 * (s + 1))
                a.wait_ge(s_gemm, W_GATE + s + 1)
                g2 = 2 * (s % 2)
                nc.scalar.activation(gT[:, 2 * s:2 * s + 2, :], bank[:, g2:g2 + 2, 0:T], ACT.Exp, scale=-1.0).then_inc(s_gexp, 1)
                if s + 1 < TS:
                    kv_load(a, 1, 2 * (s + 1) + 1)
            kv_load(a, 1, 16)
            kv_load(a, 1, 17)
            hi(W_BR + 1)
            a.wait_ge(s_logit, 1)
            nc.scalar.activation(prob[:, :], prob[:, :], ACT.Exp, bias=stat[:, 3:4], accum_out=stat[:, 4:5])
            nc.scalar.activation(stat[:, 5:6], stat[:, 1:2], ACT.Exp, bias=stat[:, 3:4]).then_inc(s_prob, 1)
            a.wait_ge(s_pT, 1)
            nc.scalar.activation(sall[:, :, 0:P], bank[:, 6:8, :].rearrange("p a (g r) -> p (a g) r", g=4), ACT.Copy).then_inc(s_pTs, 1)
            a.wait_ge(s_dps, 1)
            nc.scalar.activation(dcur[:, 0:P], bank[0:TS, 4, 0:P], ACT.Copy).then_inc(s_dcur, 1)
            npp = 0
            for c in range(KC):
                for h in range(2):
                    j = 2 * c + h
                    a.wait_ge(s_plog, j + 1)
                    o = 16 * h + 16
                    nc.scalar.activation(plog[h][:, 0:128], plog[h][:, 0:128], ACT.Exp, bias=stat[:, o + 3:o + 4], accum_out=stat[:, o + 5:o + 6])
                    nc.scalar.activation(plog[h][:, 128:384], plog[h][:, 128:384], ACT.Exp, bias=stat[:, o + 4:o + 5],
                                         accum_out=stat[:, o + 6:o + 7]).then_inc(s_pexp, 1)
                if c + 1 < TS:
                    kv_load(a, 1, 16 + 2 * (c + 1))
                for h in range(2 if c < 4 else 1):
                    npp += 1
                    a.wait_ge(s_ppT, npp)
                    if c:
                        a.wait_ge(s_po, c)
                    nc.scalar.activation(pts[h][:, :], bank[:, (7, 4)[h], 0:384], ACT.Copy).then_inc(s_pps, 1)
                if c + 1 < TS:
                    kv_load(a, 1, 16 + 2 * (c + 1) + 1)
                a.wait_ge(s_po, c + 1)
                nc.scalar.activation(work[:, c, 0:TP], bank[:, 2, 0:TP], ACT.Copy).then_inc(s_pout, 1)
            a.wait_ge(s_samp, 1)
            a.wait_ge(s_pout, KC)
            nc.scalar.activation(osq[:, :, :], work[:, 4:8, :], ACT.Square).then_inc(s_osq, 1)
            nc.scalar.activation(hhi[:, 0:4, :], work[:, 0:4, :], ACT.Copy).then_inc(s_hhi, 1)
            a.wait_ge(s_ovar, 1)
            nc.scalar.activation(osq[:, :, :], osq[:, :, :], ACT.Sqrt).then_inc(s_orstd, 1)
            a.wait_ge(s_o, 1)
            nc.scalar.activation(hhi[:, 4:8, :], work[:, 4:8, :], ACT.Copy).then_inc(s_hhi, 1)
            hi(W_BR + 2)
            hi(W_BR + 3)
            hi(W_OUT)
            hi(W_OUT + 1)
            a.wait_ge(s_mix, 1)
            nc.scalar.activation(ahi[:, 0:4, :], gT[:, 0:4, :], ACT.Copy).then_inc(s_ahi, 1)
            a.wait_ge(s_mix, 2)
            nc.scalar.activation(ahi[:, 4:8, :], gT[:, 4:8, :], ACT.Copy).then_inc(s_ahi, 1)
            hi(W_OUT + 2)
            hi(W_OUT + 3)
            hi(W_FF2)
            norm(2)
            silu.base, silu.pairs = W_FF2, NPAIR
            ff2_count = NPAIR + 2

            def act_hi2(i):
                a.wait_ge(s_act, silu.pairs + i + 1)
                nc.scalar.activation(ahi[:, bass.ds(2 * i, 2), :], act[:, :, :], ACT.Copy).then_inc(s_ahi, 1)

            def ff2_turn(i, key_i, d):
                hi(W_FF2 + 2 * i + 1, ("w", W_FF2 + 2 * key_i + 1), d)
                silu(i)
                hi(W_FF2 + 2 * i + 2, ("w", W_FF2 + 2 * key_i + 2), d)
                act_hi2(i)

            with a.Fori(0, NPAIR // 2) as i:
                ff2_turn(2 * i, 0, i)
                ff2_turn(2 * i + 1, 1, i)
            ff2_turn(NPAIR - 1, NPAIR - 1, 0)
            down(W_DN2, False)
            for cb in range(4):
                a.wait_ge(s_yT, cb + 1)
                nc.scalar.activation(yst[:, :, cb * 256:cb * 256 + 256], bank[:, 4, :].rearrange("p (a n) -> p a n", a=2), ACT.Copy).then_inc(s_ys, 1)
                nc.scalar.activation(ysts[:, cb * 256:cb * 256 + 256], bank[0:TS, 5, 0:256], ACT.Copy).then_inc(s_ys, 1)

        @block.vector
        def _(v):
            ch = Chain(v, s_vch)
            dve = nc.vector

            def lo(n, key=None, d=0, ext=0):
                key = key or ("w", n)
                s = slot_of(key)
                v.wait_ge(s_raw[s], landed(key) + 16 * d)
                v.wait_ge(s_hi, n + 1)
                w = UNIT if ext == 0 else ext
                dve.tensor_tensor(wlo[key[1] % 2][:, 0:w], raw[s][:, 0:w], whi[key[1] % 2][:, 0:w].bitcast(F32), ALU.subtract).then_inc(s_lo, 1)

            def mod_add(c):
                v.wait_ge(s_sel, c + 1)
                b = par[:, bass.ds(R_BADA + 4 * c, 4)].unsqueeze(2).broadcast_to([P, 4, 9])
                dve.tensor_tensor(mod[:, bass.ds(4 * c, 4), :], bank[:, 5, 0:36].rearrange("p (t m) -> p t m", t=4), b, ALU.add).then_inc(s_mod, 1)

            def coefficients(t, row):
                m0 = (3 * t + 1) * KC
                gain = par[:, row:row + KC].unsqueeze(2).broadcast_to([P, KC, 9])
                ch.link(dve.scalar_tensor_tensor(out=mod[:, m0:m0 + KC, :], in0=mod[:, m0:m0 + KC, :], scalar=1.0, in1=gain, op0=ALU.add, op1=ALU.mult))

            def norm(t):
                v.wait_ge(s_ssum, t + 1)
                ch.link(dve.tensor_scalar(rstd[:, 0, :], bank[:, 6, 0:T], 1.0 / D, EPS, ALU.mult, ALU.add))
                dve.reciprocal(rstd[:, 0, :], rstd[:, 0, :]).then_inc(s_var, 1)
                v.wait_ge(s_rstd, t + 1)
                sh, sc = 3 * t * KC, (3 * t + 1) * KC
                for half in range(2):
                    c0 = 4 * half
                    w = work[:, c0:c0 + 4, :]
                    ch.link(dve.tensor_tensor(w, x[:, c0:c0 + 4, :], rstd[:, 0:1, :].broadcast_to([P, 4, T]), ALU.mult))
                    for c in range(c0, c0 + 4):
                        dve.tensor_scalar(work[:, c, 0:TP], work[:, c, 0:TP], mod[:, sc + c, 0:1], mod[:, sh + c, 0:1], ALU.mult, ALU.add)
                    ws = work[:, c0:c0 + 4, TP:T]
                    ch.link(dve.tensor_tensor(ws, ws, mod[:, sc + c0:sc + c0 + 4, 1:9], ALU.mult))
                    dve.tensor_tensor(ws, ws, mod[:, sh + c0:sh + c0 + 4, 1:9], ALU.add).then_inc(s_h, 1)
                for half in range(2):
                    c0 = 4 * half
                    v.wait_ge(s_hhi, hhi_base[t] + half + 1)
                    dve.tensor_tensor(hlo[:, c0:c0 + 4, :], work[:, c0:c0 + 4, :], hhi[:, c0:c0 + 4, :].bitcast(F32), ALU.subtract).then_inc(s_hlo, 1)

            hhi_base = (0, 2, 6)

            def act_mul(i):
                v.wait_ge(s_sil, act_mul.pairs + i + 1)
                v.wait_ge(s_gemm, act_mul.base + 2 * i + 2)
                dve.tensor_tensor(act[:, :, :], sil[:, :, :], bank[:, 2:4, 0:T], ALU.mult).then_inc(s_act, 1)

            def act_lo(i):
                v.wait_ge(s_ahi, act_mul.ahi + i + 1)
                dve.tensor_tensor(alo[:, bass.ds(2 * i, 2), :], act[:, :, :], ahi[:, bass.ds(2 * i, 2), :].bitcast(F32), ALU.subtract).then_inc(s_alo, 1)

            def x_update(b, m0, gate):
                g = gate * KC + m0
                if x_update.n:
                    v.wait_ge(s_xup, x_update.n)
                x_update.n += 1
                ch.link(dve.tensor_tensor(tmps[:, :, :], bank[:, b:b + 2, TP:T], mod[:, g:g + 2, 1:9], ALU.mult))
                for t in range(2):
                    dve.scalar_tensor_tensor(out=x[:, m0 + t, 0:TP], in0=bank[:, b + t, 0:TP], scalar=mod[:, g + t, 0:1], in1=x[:, m0 + t, 0:TP],
                                             op0=ALU.mult, op1=ALU.add)
                dve.tensor_tensor(x[:, m0:m0 + 2, TP:T], x[:, m0:m0 + 2, TP:T], tmps[:, :, :], ALU.add).then_inc(s_xup, 1)

            x_update.n = 0
            ch.link(dve.memset(csilu[:, :, :], 0.0))
            dve.memset(misc[:, :], 0.0).then_inc(s_zero, 1)
            v.wait_ge(s_parT, 1)
            dve.tensor_copy(par[:, :], bank[:, 7, 0:NROWS]).then_inc(s_par, 1)
            v.wait_ge(s_par, 1)
            v.wait_ge(s_const, 16)
            v.wait_ge(s_zero, 1)
            ch.link(dve.tensor_tensor(misc[:, 0:1], par[:, R_LQ:R_LQ + 1], par[:, R_LK:R_LK + 1], ALU.mult))
            dve.tensor_scalar(misc[:, 2:4], C("half"), misc[:, 0:1], None, ALU.mult).then_inc(s_par, 1)
            ch.link(dve.tensor_scalar(misc[:, 8:9], par[:, R_QNA:R_QNA + 1], 0.125, None, ALU.mult))
            ch.link(dve.tensor_scalar(misc[:, 9:10], par[:, R_QNB:R_QNB + 1], 0.125, None, ALU.mult))
            ch.link(dve.tensor_copy(misc[:, 10:11], par[:, R_KNA:R_KNA + 1]))
            ch.link(dve.tensor_copy(misc[:, 11:12], par[:, R_KNB:R_KNB + 1]))
            ch.link(dve.tensor_scalar(misc[:, 12:13], par[:, R_SUB:R_SUB + 1], 1.0 - LAM_INIT, None, ALU.mult))
            for r2 in range(2):
                v.wait_ge(s_xT, r2 + 1)
                dve.tensor_copy(x[:, 4 * r2:4 * r2 + 4, :], bank[:, 0:4, 0:T]).then_inc(s_xfirst, 1)
            v.wait_ge(s_lamexp, 1)
            ch.link(dve.tensor_tensor(misc[:, 6:7], misc[:, 5:6], misc[:, 4:5], ALU.subtract))
            ch.link(dve.tensor_scalar(misc[:, 6:7], misc[:, 6:7], -LAM_INIT, None, ALU.add))
            ch.link(dve.tensor_scalar(misc[:, 7:8], C("coeflam"), misc[:, 6:7], C("coef1"), ALU.mult, ALU.add))
            for c in range(ADA_PRO):
                mod_add(c)
            v.wait_ge(s_mod, ADA_PRO)
            coefficients(0, R_N1)
            lo(W_FF1)
            norm(0)
            act_mul.base, act_mul.pairs, act_mul.ahi = W_FF1, 0, 0

            def ff1_turn(i, key_i, d):
                lo(W_FF1 + 2 * i + 1, ("w", W_FF1 + 2 * key_i + 1), d)
                lo(W_FF1 + 2 * i + 2, ("w", W_FF1 + 2 * key_i + 2), d)
                act_mul(i)
                act_lo(i)
                mod_add(ADA_PRO + i)

            ff1_turn(0, 0, 0)
            with v.Fori(1, NPAIR) as i:
                ff1_turn(i, 1, i - 1)

            def down(first, gate, ada):
                for u in range(12):
                    n = first + u
                    if u:
                        lo(n, ext=width_of(n))
                    if ada and u == 0:
                        v.wait_ge(s_mod, 6)
                        ch.link(dve.tensor_scalar(mod[:, 2 * KC:3 * KC, :], mod[:, 2 * KC:3 * KC, :], 0.5, None, ALU.mult))
                    if ada and u == 7:
                        mod_add(ADA_PRO + NPAIR)
                    if u % 3 == 1 and u > 3:
                        cb = u // 3 - 1
                        v.wait_ge(s_gemm, first + 3 * cb + 3)
                        x_update(2 * (cb % 2), 2 * cb, gate)
                if ada:
                    v.wait_ge(s_mod, 10)
                    coefficients(1, R_N2)
                lo(first + 12) if first == W_DN1 else None
                v.wait_ge(s_gemm, first + 12)
                x_update(2, 6, gate)

            down(W_DN1, 2, True)
            norm(1)
            mod_add(ADA_PRO + NPAIR + 1)

            nk = 0
            tk = 0

            def head_norm(u):
                ab, kind, p = u // 6, u % 6 // 2, u % 2
                v.wait_ge(s_nsum, nk)
                if nk > 1:
                    v.wait_ge(s_qk, nk - 1)
                ch.link(dve.tensor_scalar(rstd[:, :, :], bank[:, 6:8, 0:T], 1.0 / 64, EPS, ALU.mult, ALU.add))
                dve.reciprocal(rstd[:, :, :], rstd[:, :, :]).then_inc(s_nvar, 1)
                v.wait_ge(s_nrstd, nk)
                dst = (qT, kT)[kind][:, 4 * ab + 2 * p:4 * ab + 2 * p + 2, :]
                g = 8 + 2 * kind + ab
                dve.scalar_tensor_tensor(out=dst, in0=dst, scalar=misc[:, g:g + 1], in1=rstd[:, :, :], op0=ALU.mult, op1=ALU.mult).then_inc(s_qk, 1)

            def tokens(u):
                ab, kind, p = u // 6, u % 6 // 2, u % 2
                v.wait_ge(s_turn, tk)
                f0 = 512 * ab + 256 * p
                if kind == 1 and tk > 1:
                    v.wait_ge(s_rowout, 32 * (tk - 1))
                dst = kst[:, :, :] if kind == 1 else vtok[:, :, f0:f0 + 256]
                dsts = ksts[:, :] if kind == 1 else vtoks[:, f0:f0 + 256]
                dve.tensor_copy(dst, bank[:, 4, :].rearrange("p (a n) -> p a n", a=2)).then_inc(s_tok, 1)
                dve.tensor_copy(dsts, bank[0:TS, 5, 0:256]).then_inc(s_tok, 1)

            for u in range(12):
                lo(W_QKV + u + 1)
                if u > 0:
                    w = (u - 1) % 6 // 2
                    if w < 2:
                        nk += 1
                        head_norm(u - 1)
                    if w > 0:
                        tk += 1
                        tokens(u - 1)
                if u == 7:
                    mod_add(ADAC - 1)
            tk += 1
            tokens(11)
            v.wait_ge(s_mod, ADAC)
            coefficients(2, R_N3)
            ch.link(dve.tensor_scalar(mod[:, 8 * KC:9 * KC, :], mod[:, 8 * KC:9 * KC, :], 0.5, None, ALU.mult))

            def sigmoid(s):
                v.wait_ge(s_gexp, s + 1)
                g = gT[:, 2 * s:2 * s + 2, :]
                ch.link(dve.tensor_scalar(g, g, 1.0, None, ALU.add))
                dve.reciprocal(g, g).then_inc(s_sig, 1)

            for s in range(TS):
                if s < TS:
                    n = W_GATE + s + 1
                    lo(n, ext=width_of(n))
                for half in range(2):
                    for ab in range(2):
                        use = 2 * s + half
                        v.wait_ge(s_mul, 4 * s + 2 * half + ab + 1)
                        r0 = 16 * s + 8 * ab
                        dve.tensor_reduce(sall[:, 4 * half:4 * half + 4, r0:r0 + 8],
                                          kv[ab][use % 2][:, :, :].rearrange("p g (h d) -> p g h d", d=64), AX.X, ALU.add).then_inc(s_red, 1)
                    if half == 0 and s:
                        sigmoid(s - 1)
            sigmoid(TS - 1)
            lo(W_BR + 1)

            v.wait_ge(s_red, 4 * TS)
            prod = work[:, 0, 0:64].rearrange("p (c s) -> p c s", c=KC)
            ch.link(dve.tensor_tensor(prod, qT[:, :, TP:T], kT[:, :, TP:T], ALU.mult))
            ev = ecur[:, :].rearrange("p (s c h) -> p s c h", s=TS, h=2)
            for h in range(2):
                ins = dve.tensor_scalar(ev[:, :, :, h], prod.rearrange("p c s -> p s c"), C("half", h, h + 1), None, ALU.mult)
            ins.then_inc(s_ecur, 1)
            dve.memset(dcur[:, :], 0.0)
            ch.link(dve.tensor_scalar(b0[:, :], C("distrow"), C("negslope"), None, ALU.mult))
            v.wait_ge(s_lT, 1)
            blk = stat[:, 8:12]
            ch.link(dve.tensor_reduce(blk, bank[:, 4:6, :].rearrange("p a (b n) -> p (a b) n", n=256), AX.X, ALU.add))
            bm = blk.unsqueeze(1).broadcast_to([P, 4, 4])
            bn = blk.unsqueeze(2).broadcast_to([P, 4, 4])
            gt = stat[:, 16:32].rearrange("p (n m) -> p n m", n=4)
            eq = stat[:, 32:48].rearrange("p (n m) -> p n m", n=4)
            ch.link(dve.tensor_tensor(gt, bm, bn, ALU.is_gt))
            ch.link(dve.tensor_tensor(eq, bm, bn, ALU.is_equal))
            ch.link(dve.tensor_tensor(eq, eq, C("tri").rearrange("p (n m) -> p n m", n=4), ALU.mult))
            ch.link(dve.tensor_tensor(gt, gt, eq, ALU.add))
            ch.link(dve.tensor_reduce(stat[:, 12:16], gt, AX.X, ALU.add))
            ch.link(dve.tensor_scalar(stat[:, 12:16], stat[:, 12:16], 2.5, -BIG, ALU.is_gt, ALU.mult))
            ch.link(dve.tensor_scalar(stat[:, 12:16], stat[:, 12:16], C("rowA"), None, ALU.mult))
            pen = stat[:, 12:16].unsqueeze(2).broadcast_to([P, 4, 2])
            ch.link(dve.tensor_tensor(stat[:, 48:56].rearrange("p (b g) -> p b g", b=4), C("pageslope").rearrange("p (b g) -> p b g", b=4), pen, ALU.add))
            for g in range(NPG):
                ins = dve.scalar_tensor_tensor(out=prob[:, 128 * g:128 * g + 128], in0=bank[:, 4 + g // 4, 128 * (g % 4):128 * (g % 4) + 128],
                                               scalar=stat[:, 48 + g:49 + g], in1=b0[:, :], op0=ALU.add, op1=ALU.add)
            ch.link(ins)
            ch.link(dve.tensor_reduce(stat[:, 2:3], prob[:, :], AX.X, ALU.max))
            v.wait_ge(s_cur, 1)
            ch.link(dve.tensor_copy(stat[:, 1:2], bank[:, 6, 0:1]))
            ch.link(dve.tensor_tensor(stat[:, 2:3], stat[:, 2:3], stat[:, 1:2], ALU.max))
            dve.tensor_scalar(stat[:, 3:4], stat[:, 2:3], -1.0, None, ALU.mult).then_inc(s_logit, 1)
            v.wait_ge(s_prob, 1)
            ch.link(dve.tensor_tensor(stat[:, 6:7], stat[:, 4:5], stat[:, 5:6], ALU.add))
            ch.link(dve.reciprocal(stat[:, 6:7], stat[:, 6:7]))
            ch.link(dve.tensor_tensor(stat[:, 6:7], stat[:, 6:7], misc[:, 7:8], ALU.mult))
            dve.tensor_scalar(prob[:, :], prob[:, :], stat[:, 6:7], None, ALU.mult).then_inc(s_pscaled, 1)
            ch.link(dve.tensor_tensor(stat[:, 5:6], stat[:, 5:6], stat[:, 6:7], ALU.mult))
            dve.tensor_scalar(ecur[:, :], ident, stat[:, 5:6], None, ALU.mult).then_inc(s_diag, 1)
            v.wait_ge(s_lT, 1)
            dve.memset(sall[:, :, P:RW], 0.0).then_inc(s_diag, 1)

            v.wait_ge(s_pT, 1)
            for c in range(KC):
                for h in range(2):
                    j = 2 * c + h
                    v.wait_ge(s_psc, j + 1)
                    o = 16 * h + 16
                    dve_l = plog[h][:, :]
                    if c:
                        v.wait_ge(s_ppT, min(2 * c, 8) + max(c - 4, 0))
                    ch.link(dve.scalar_tensor_tensor(out=dve_l, in0=C("dist"), scalar=-slope_of_row(j), in1=bank[:, 5 + h, 0:384], op0=ALU.mult, op1=ALU.add))
                    ch.link(dve.tensor_reduce(stat[:, o:o + 3], dve_l.rearrange("p (a n) -> p a n", n=128), AX.X, ALU.max))
                    ch.link(dve.tensor_tensor(stat[:, o + 1:o + 2], stat[:, o + 1:o + 2], stat[:, o + 2:o + 3], ALU.max))
                    dve.tensor_scalar(stat[:, o + 3:o + 5], stat[:, o:o + 2], -1.0, None, ALU.mult).then_inc(s_plog, 1)
                for h in range(2):
                    j = 2 * c + h
                    o = 16 * h + 16
                    v.wait_ge(s_pexp, j + 1)
                    ch.link(dve.reciprocal(stat[:, o + 8:o + 10], stat[:, o + 5:o + 7]))
                    if c >= 4 and h == 1:
                        ch.link(dve.tensor_scalar(stat[:, o + 8:o + 10], stat[:, o + 8:o + 10], misc[:, 6:7], None, ALU.mult))
                    for seg, (e0, e1) in enumerate(((0, 128), (128, 384))):
                        pr = plog[h][:, e0:e1]
                        r_ = stat[:, o + 8 + seg:o + 9 + seg]
                        if c >= 4 and h == 1:
                            ins = dve.scalar_tensor_tensor(out=plog[0][:, e0:e1], in0=pr, scalar=r_, in1=plog[0][:, e0:e1], op0=ALU.mult, op1=ALU.add)
                        else:
                            ins = dve.tensor_scalar(pr, pr, r_, None, ALU.mult)
                    ins.then_inc(s_pscale, 1)
                    if c >= 4 and h == 0:
                        v.wait_ge(s_pscale, j + 1)
                v.wait_ge(s_pvd, c + 1)
                if c:
                    v.wait_ge(s_ext, c)
                dve.tensor_tensor(om[:, 0, :], bank[:, 0, :], C("maskA"), ALU.mult)
                dve.tensor_tensor(om[:, 1, :], bank[:, 1, :], C("maskB"), ALU.mult).then_inc(s_om, 1)
            v.wait_ge(s_ext, TS)
            dve.tensor_copy(work[:, :, TP:T], bank[:, 3, 0:64].rearrange("p (c s) -> p c s", c=KC)).then_inc(s_samp, 1)
            v.wait_ge(s_pout, KC)
            v.wait_ge(s_osum, 1)
            ch.link(dve.tensor_scalar(osq[:, :, :], bank[:, 4:8, 0:T], 1.0 / P, EPS, ALU.mult, ALU.add))
            dve.reciprocal(osq[:, :, :], osq[:, :, :]).then_inc(s_ovar, 1)
            v.wait_ge(s_hhi, 5)
            dve.tensor_tensor(hlo[:, 0:4, :], work[:, 0:4, :], hhi[:, 0:4, :].bitcast(F32), ALU.subtract).then_inc(s_hlo, 1)
            v.wait_ge(s_orstd, 1)
            dve.scalar_tensor_tensor(out=work[:, 4:8, :], in0=work[:, 4:8, :], scalar=misc[:, 12:13], in1=osq[:, :, :], op0=ALU.mult, op1=ALU.mult).then_inc(s_o, 1)
            v.wait_ge(s_hhi, 6)
            dve.tensor_tensor(hlo[:, 4:8, :], work[:, 4:8, :], hhi[:, 4:8, :].bitcast(F32), ALU.subtract).then_inc(s_hlo, 1)
            lo(W_BR + 2)
            lo(W_BR + 3)
            v.wait_ge(s_sig, TS)
            for half in range(2):
                for ab in range(2):
                    v.wait_ge(s_gemm, W_BR + 2 * half + ab + 1)
                    g = gT[:, 8 * ab + 4 * half:8 * ab + 4 * half + 4, :]
                    ch.link(dve.tensor_tensor(g, bank[:, 4 * ab:4 * ab + 4, 0:T], g, ALU.mult))
                ga, gb = gT[:, 4 * half:4 * half + 4, :], gT[:, 8 + 4 * half:12 + 4 * half, :]
                dve.tensor_tensor(ga, ga, gb, ALU.add).then_inc(s_mix, 1)
            lo(W_OUT)
            lo(W_OUT + 1)
            for half in range(2):
                v.wait_ge(s_ahi, NPAIR + half + 1)
                dve.tensor_tensor(alo[:, 4 * half:4 * half + 4, :], gT[:, 4 * half:4 * half + 4, :], ahi[:, 4 * half:4 * half + 4, :].bitcast(F32),
                                  ALU.subtract).then_inc(s_alo, 1)
            for cb in range(4):
                if cb < 2:
                    lo(W_OUT + 2 + cb)
                elif cb == 2:
                    lo(W_FF2)
                v.wait_ge(s_gemm, W_OUT + cb + 1)
                x_update(2 * (cb % 2), 2 * cb, 5)
            norm(2)
            act_mul.base, act_mul.pairs, act_mul.ahi = W_FF2, NPAIR, NPAIR + 2

            def act_lo2(i):
                v.wait_ge(s_ahi, NPAIR + 2 + i + 1)
                dve.tensor_tensor(alo[:, bass.ds(2 * i, 2), :], act[:, :, :], ahi[:, bass.ds(2 * i, 2), :].bitcast(F32), ALU.subtract).then_inc(s_alo, 1)

            def ff2_turn(i, key_i, d):
                lo(W_FF2 + 2 * i + 1, ("w", W_FF2 + 2 * key_i + 1), d)
                lo(W_FF2 + 2 * i + 2, ("w", W_FF2 + 2 * key_i + 2), d)
                act_mul(i)
                act_lo2(i)

            with v.Fori(0, NPAIR // 2) as i:
                ff2_turn(2 * i, 0, i)
                ff2_turn(2 * i + 1, 1, i)
            ff2_turn(NPAIR - 1, NPAIR - 1, 0)
            down(W_DN2, 8, False)

        @block.tensor
        def _(pe):
            mm = nc.tensor.matmul

            def product(b, slot, k, w, col, xh, xl, start, stop):
                wh = whi[slot][:, k * w + col:k * w + col + P]
                wl = wlo[slot][:, k * w + col:k * w + col + P]
                out = bank[:, b, 0:T]
                mm(out, wh, xh, start=start, stop=False)
                mm(out, wh, xl, start=False, stop=False)
                return mm(out, wl, xh, start=False, stop=stop)

            def tile_product(b, n, parity, t, xh, xl, nk=KC, w=256, k0=0, first=True, last=True, signal=False):
                for k in range(nk):
                    ins = product(b, parity, k, w, t * P, xh[:, k0 + k, :], xl[:, k0 + k, :], first and k == 0, last and k == nk - 1)
                if signal:
                    ins.then_inc(s_gemm, 1)

            def split_ready(n):
                pe.wait_ge(s_hi, n + 1)
                pe.wait_ge(s_lo, n + 1)

            def ada(c, key_c=None, d=0):
                key_c = c if key_c is None else key_c
                if not (isinstance(c, int) and c == 0):
                    pe.wait_ge(s_adarow, c)
                for half in range(2):
                    key = ("ada", key_c, half)
                    s = slot_of(key)
                    pe.wait_ge(s_raw[s], landed(key) + 16 * d)
                    for j in range(4):
                        ins = mm(bank[32 * j:32 * j + 32, 4, :], csilu[:, 4 * half + j, :], raw[s][:, 512 * j:512 * j + 512], start=(half == 0), stop=(half == 1))
                ins.then_inc(s_ada, 1)

            def ada_turn(c):
                pe.wait_ge(s_adarow, c + 1)
                if not (isinstance(c, int) and c == 0):
                    pe.wait_ge(s_mod, c)
                for t in range(4):
                    ins = mm(bank[:, 5, 9 * t:9 * t + 9], adarow[:, P * t:P * t + P], C("sel9"), start=True, stop=True)
                ins.then_inc(s_sel, 1)

            def norm(t):
                pe.wait_ge(s_sq, t + 1)
                for c in range(KC):
                    ins = mm(bank[:, 6, 0:T], C("ones"), work[:, c, :], start=(c == 0), stop=(c == KC - 1))
                ins.then_inc(s_ssum, 1)

            pe.wait_ge(s_const, 16)
            pe.wait_ge(s_rows, 16)
            pe.wait_ge(s_crow, 16)
            nc.tensor.transpose(bank[:, 7, 0:NROWS], rows[:, :], ident[0:NROWS, 0:NROWS])
            nc.tensor.transpose(bank[:, 6, 0:72], crow[:, :], ident[0:72, 0:72]).then_inc(s_parT, 1)
            pe.wait_ge(s_x, 32)
            for r2 in range(2):
                if r2:
                    pe.wait_ge(s_xfirst, 1)
                for q in range(4):
                    c = 4 * r2 + q
                    for tt in range(2):
                        nc.tensor.transpose(bank[:, q, P * tt:P * tt + P], xtok[:, tt, P * c:P * c + P], ident)
                    ins = nc.tensor.transpose(bank[:, q, TP:T], xtoks[:, P * c:P * c + P], ident[0:TS, 0:TS])
                ins.then_inc(s_xT, 1)
            pe.wait_ge(s_par, 2)
            pe.wait_ge(s_csilu, 1)
            mm(bank[:, 6, 0:2], C("ones"), misc[:, 2:4], start=True, stop=True).then_inc(s_lamsum, 1)
            for c in range(ADA_PRO):
                ada(c)
                ada_turn(c)
            pe.wait_ge(s_lamexp, 1)
            norm(0)

            def ff_pair(i, n, pairs):
                split_ready(n)
                if not (isinstance(i, int) and i + pairs == 0):
                    pe.wait_ge(s_sil, pairs + i)
                for t in range(2):
                    tile_product(t, n, 0, t, hhi, hlo, signal=(t == 1))

            def ff_up(i, n, pairs):
                split_ready(n)
                if not (isinstance(i, int) and i + pairs == 0):
                    pe.wait_ge(s_act, pairs + i)
                for t in range(2):
                    tile_product(2 + t, n, 1, t, hhi, hlo, signal=(t == 1))

            pe.wait_ge(s_hlo, 2)

            def ff1_turn(i, key_i, d):
                ff_pair(i, W_FF1 + 2 * i, 0)
                ada(ADA_PRO + i, ADA_PRO + key_i, d)
                ff_up(i, W_FF1 + 2 * i + 1, 0)
                ada_turn(ADA_PRO + i)

            ff1_turn(0, 0, 0)
            with pe.Fori(1, NPAIR) as i:
                ff1_turn(i, 1, i - 1)

            def down(first, pairs, ahis, xups, with_ada):
                pe.wait_ge(s_alo, ahis)
                for cb in range(4):
                    for third in range(3):
                        n = first + 3 * cb + third
                        split_ready(n)
                        if third == 0:
                            if cb == 0:
                                pe.wait_ge(s_sil, pairs)
                            elif cb == 1:
                                pe.wait_ge(s_act, pairs)
                            else:
                                pe.wait_ge(s_xup, xups + cb - 1)
                        nk = min(FC - 8 * third, 8)
                        for t in range(2):
                            tile_product(2 * (cb % 2) + t, n, n % 2, t, ahi, alo, nk=nk, k0=8 * third, first=(third == 0), last=(third == 2), signal=(t == 1))
                        if with_ada and (cb, third) == (1, 2):
                            ada(ADA_PRO + NPAIR)
                        if with_ada and (cb, third) == (2, 0):
                            ada_turn(ADA_PRO + NPAIR)
                if with_ada:
                    ada(ADA_PRO + NPAIR + 1)

            down(W_DN1, NPAIR, NPAIR, 0, True)
            norm(1)
            ada_turn(ADA_PRO + NPAIR + 1)

            nk = tk = 0
            pe.wait_ge(s_hlo, 4)
            for u in range(13):
                n = W_QKV + u
                if u < 12:
                    split_ready(n)
                    if u >= 2:
                        pe.wait_ge(s_proj, u - 1)
                    else:
                        pe.wait_ge(s_xup, 4)
                    tile_product(2 * (u % 2), n, n % 2, 0, hhi, hlo)
                w = u - 1
                kind = w % 6 // 2
                if u > 0 and kind < 2:
                    pe.wait_ge(s_proj, w + 1)
                    if nk:
                        pe.wait_ge(s_nvar, nk)
                    for t in range(2):
                        ins = mm(bank[:, 6 + t, 0:T], C("blockdiag"), sqb[:, t, :], start=True, stop=True)
                    ins.then_inc(s_nsum, 1)
                    nk += 1
                if u < 12:
                    tile_product(2 * (u % 2) + 1, n, n % 2, 1, hhi, hlo, signal=True)
                if u == 7:
                    pass
                if u > 0 and kind > 0:
                    ab, p = w // 6, w % 2
                    if kind == 1:
                        pe.wait_ge(s_qk, nk)
                    else:
                        pe.wait_ge(s_proj, w + 1)
                    if tk:
                        pe.wait_ge(s_tok, 2 * tk)
                    if tk == 4:
                        pe.wait_ge(s_mod, ADAC)
                    for t in range(2):
                        src = kT[:, 4 * ab + 2 * p + t, :] if kind == 1 else vT[:, t, :]
                        for tt in range(2):
                            nc.tensor.transpose(bank[:, 4, 256 * tt + P * t:256 * tt + P * t + P], src[:, P * tt:P * tt + P], ident)
                        ins = nc.tensor.transpose(bank[0:TS, 5, P * t:P * t + P], src[:, TP:T], ident)
                    ins.then_inc(s_turn, 1)
                    tk += 1
                if u == 6:
                    pe.wait_ge(s_tok, 8)
                    ada(ADAC - 1)
                    ada_turn(ADAC - 1)

            for s in range(TS):
                if s == 0:
                    pe.wait_ge(s_qk, 8)
                    pe.wait_ge(s_tok, 16)
                elif s >= 2:
                    pe.wait_ge(s_qb, s - 1)
                for c in range(KC):
                    ins = mm(bank[:, 4 + 2 * (s % 2) + c // 4, P * (c % 4):P * (c % 4) + P], qT[:, c, TP + s:TP + s + 1].broadcast_to([P, P]), ident,
                             start=True, stop=True)
                ins.then_inc(s_qbp, 1)
                n = W_GATE + s
                split_ready(n)
                if s >= 2:
                    pe.wait_ge(s_gexp, s - 1)
                else:
                    pe.wait_ge(s_proj, 11 + s)
                for t in range(2):
                    tile_product(2 * (s % 2) + t, n, n % 2, t, hhi, hlo, signal=(t == 1))

            pe.wait_ge(s_red, 4 * TS)
            pe.wait_ge(s_qb, TS)
            for g in range(NPG):
                ins = nc.tensor.transpose(bank[:, 4 + g // 4, P * (g % 4):P * (g % 4) + P], sall[:, g, 0:P], ident)
            ins.then_inc(s_lT, 1)
            pe.wait_ge(s_ecur, 1)
            mm(bank[:, 6, 0:1], ecur[:, :], C("ones", 0, 1), start=True, stop=True).then_inc(s_cur, 1)
            pe.wait_ge(s_pscaled, 1)
            for g in range(NPG):
                ins = nc.tensor.transpose(bank[:, 6 + g // 4, P * (g % 4):P * (g % 4) + P], prob[:, P * g:P * g + P], ident)
            ins.then_inc(s_pT, 1)
            pe.wait_ge(s_diag, 2)
            mm(bank[0:TS, 4, 0:P], C("sel8"), ecur[:, :], start=True, stop=True).then_inc(s_dps, 1)

            npp = 0
            pe.wait_ge(s_gexp, TS)
            pe.wait_ge(s_pTs, 1)
            pe.wait_ge(s_dcur, 1)
            for c in range(KC):
                for h in range(2):
                    if c:
                        pe.wait_ge(s_plog, 2 * c)
                    r0, r1 = 64 * h, 64 * h + 64
                    mm(bank[:, 5 + h, 0:128], qT[r0:r1, c, 0:128], kT[r0:r1, c, 0:128], start=True, stop=True)
                    mm(bank[:, 5 + h, 128:384], qT[r0:r1, c, 128:256], kT[r0:r1, c, 0:256], start=True, stop=True).then_inc(s_psc, 1)
                if c:
                    pe.wait_ge(s_om, c)
                for half in range(2):
                    for ab in range(2):
                        use = 16 + 2 * c + half
                        pe.wait_ge(s_kv[ab][use % 2], kv_landed(use))
                        r0 = 16 * c + 8 * ab
                        for q in range(4):
                            ins = mm(bank[32 * q:32 * q + 32, ab, :], sall[:, 4 * half + q, r0:r0 + 32], kv[ab][use % 2][:, q, :],
                                     start=(half == 0), stop=(half == 1 and q > 0))
                        ins.then_inc(s_pv, 1)
                for ab in range(2):
                    r0 = 16 * c + 8 * ab
                    ins = mm(bank[0:32, ab, :], dcur[:, r0:r0 + 32], vtoks[:, 512 * ab:512 * ab + 512], start=False, stop=True)
                ins.then_inc(s_pvd, 1)
                for h in range(2 if c < 4 else 1):
                    pe.wait_ge(s_pscale, 2 * c + (h + 1 if c < 4 else 2))
                    b = (7, 4)[h]
                    if npp:
                        pe.wait_ge(s_pps, npp)
                    for e in range(3):
                        ins = nc.tensor.transpose(bank[:, b, P * (0, 1, 2)[e]:P * (0, 1, 2)[e] + P], plog[h][:, P * e:P * e + P], ident)
                    ins.then_inc(s_ppT, 1)
                    npp += 1
                pe.wait_ge(s_om, c + 1)
                for f in range(KC):
                    ins = mm(bank[:, 3, TS * f + c:TS * f + c + 1], om[:, f // 4, P * (f % 4):P * (f % 4) + P], C("ones", 0, 1), start=True, stop=True)
                ins.then_inc(s_ext, 1)
                pe.wait_ge(s_pps, npp)
                if c:
                    pe.wait_ge(s_pout, c)
                for h in range(2 if c < 4 else 1):
                    wd = 64 if c < 4 else 128
                    v0 = P * c + 64 * h
                    out = bank[64 * h:64 * h + wd, 2, :]
                    mm(out[:, 0:TP], vtok[:, 0, v0:v0 + wd], pts[h][:, 0:256], start=True, stop=False)
                    ins = mm(out[:, 128:TP], vtok[:, 1, v0:v0 + wd], pts[h][:, 256:384], start=False, stop=True)
                ins.then_inc(s_po, 1)
            pe.wait_ge(s_osq, 1)
            pe.wait_ge(s_pps, npp)
            for q in range(4):
                ins = mm(bank[:, 4 + q, 0:T], C("ones"), osq[:, q, :], start=True, stop=True)
            ins.then_inc(s_osum, 1)

            pe.wait_ge(s_hlo, 6)
            for q in range(4):
                n = W_BR + q
                ab, half = q % 2, q // 2
                split_ready(n)
                if half:
                    pe.wait_ge(s_mix, 1)
                for t in range(4):
                    tile_product(4 * ab + t, n, n % 2, t, hhi, hlo, nk=4, w=512, k0=4 * ab, signal=(t == 3))
            pe.wait_ge(s_alo, NPAIR + 2)
            for cb in range(4):
                n = W_OUT + cb
                split_ready(n)
                if cb >= 2:
                    pe.wait_ge(s_xup, 4 + cb - 1)
                for t in range(2):
                    tile_product(2 * (cb % 2) + t, n, n % 2, t, ahi, alo, signal=(t == 1))
            norm(2)
            pe.wait_ge(s_hlo, 8)
            pe.wait_ge(s_xup, 8)

            with pe.Fori(0, NPAIR // 2) as i:
                for q in range(2):
                    j = 2 * i + q
                    ff_pair(j, W_FF2 + 2 * j, NPAIR)
                    ff_up(j, W_FF2 + 2 * j + 1, NPAIR)
            ff_pair(NPAIR - 1, W_FF2 + 2 * NPAIR - 2, NPAIR)
            ff_up(NPAIR - 1, W_FF2 + 2 * NPAIR - 1, NPAIR)
            down(W_DN2, 2 * NPAIR, 2 * NPAIR + 2, 8, False)
            for cb in range(4):
                pe.wait_ge(s_xup, 8 + cb + 1)
                if cb:
                    pe.wait_ge(s_ys, 2 * cb)
                for t in range(2):
                    for tt in range(2):
                        nc.tensor.transpose(bank[:, 4, 256 * tt + P * t:256 * tt + P * t + P], x[:, 2 * cb + t, P * tt:P * tt + P], ident)
                    ins = nc.tensor.transpose(bank[0:TS, 5, P * t:P * t + P], x[:, 2 * cb + t, TP:T], ident)
                ins.then_inc(s_yT, 1)


OUTS = [("y_prompt", (1, TP, D)), ("y_sample", (TS, 1, D)),
        ("k_moba_prompt", (1, 1, TP, 8, 64)), ("v_moba_prompt", (1, 1, TP, 8, 64)),
        ("k_diff_prompt", (1, 1, TP, 4, 128)), ("v_diff_prompt", (1, 1, TP, 4, 128)),
        ("k_moba_sample", (1, TS, 1, 8, 64)), ("v_moba_sample", (1, TS, 1, 8, 64)),
        ("k_diff_sample", (1, TS, 1, 4, 128)), ("v_diff_sample", (1, TS, 1, 4, 128))]
DIRECT = ["x_prompt", "x_sample", "cache_k_moba", "cache_v_moba", "cache_k_diff", "cache_v_diff", "page_table", "w_ada",
          "ffn1_w_gate", "ffn1_w_up", "ffn1_w_down", "w_in", "w_branch_moba", "w_branch_diff", "w_out",
          "ffn2_w_gate", "ffn2_w_up", "ffn2_w_down"]


def kernel(**inputs):
    import concourse.bacc as bacc
    from concourse.bass_utils import run_bass_kernel_spmd

    g = {k: np.asarray(v) for k, v in inputs.items()}
    arrays = {k: np.ascontiguousarray(g[k]) for k in DIRECT}
    arrays["params"] = np.concatenate([
        g["b_ada"].reshape(72, P), g["norm_ffn1"].reshape(8, P), g["norm_mix"].reshape(8, P), g["norm_ffn2"].reshape(8, P)]
        + [np.concatenate([g[n], g[n]], 1) for n in ("qn_moba", "kn_moba", "qn_diff", "kn_diff")]
        + [g["subln_diff"], np.concatenate([g["lambda_q1"], g["lambda_q2"]], 1), np.concatenate([g["lambda_k1"], g["lambda_k2"]], 1)], 0)
    c9 = np.concatenate([g["c_prompt"], g["c_sample"]], 0)
    arrays["c_rows"] = np.ascontiguousarray(c9.reshape(9, KC, P).transpose(1, 0, 2)).reshape(72, P)
    arrays["consts"] = constants()

    nc = bacc.Bacc("TRN2", target_bir_lowering=False, num_devices=1)
    A = {k: nc.dram_tensor(f"in_{k}", a.shape, mybir.dt.from_np(a.dtype), kind="ExternalInput").ap() for k, a in arrays.items()}
    O = {k: nc.dram_tensor(f"out_{k}", s, F32, kind="ExternalOutput").ap() for k, s in OUTS}
    build(nc, A, O)
    r = run_bass_kernel_spmd(nc, [{f"in_{k}": a for k, a in arrays.items()}], core_ids=[0])
    return tuple(r.results[0][f"out_{k}"] for k, _ in OUTS)
```

```python
from contextlib import ExitStack

import numpy as np
import concourse.bass as bass
from concourse import mybir

F32 = mybir.dt.float32
F32R = mybir.dt.float32r
I32 = mybir.dt.int32
ALU = mybir.AluOpType
ACT = mybir.ActivationFunctionType
AX = mybir.AxisListType

P = 128
D = 1024
KC = D // P
TP = 256
TS = 8
T = TP + TS
FF = 2816
FC = FF // P
NPAIR = FC // 2
NMOD = 9
PAST = 1024
PAGE = 128
NPG = PAST // PAGE
NPHYS = 80
EPS = 1e-6
LAM_INIT = 0.2
UNIT = 2048
SLOTS = 4
ADAC = NMOD * D // 512
KVS = 3
RW = 152
BIG = 1e30

W_FF1, W_DN1 = 0, 22
W_QKV, W_GATE, W_BR, W_OUT = 34, 46, 54, 58
W_FF2, W_DN2 = 62, 84
ADA_PRO = 4


def stream_plan():
    plan = []
    ada = lambda c: [("ada", c, 0), ("ada", c, 1)]
    for c in range(ADA_PRO):
        plan += ada(c)
    for i in range(NPAIR):
        plan += [("w", W_FF1 + 2 * i)] + ada(ADA_PRO + i) + [("w", W_FF1 + 2 * i + 1)]
    for i in range(3):
        plan += [("w", W_DN1 + 4 * i + u) for u in range(4)] + ada(ADA_PRO + NPAIR + i)
    plan += [("w", n) for n in range(W_QKV, W_DN2 + 12)]
    return plan


PLAN = stream_plan()


def slots():
    where, fills, before = {}, {}, {}
    last = [None] * SLOTS
    age, count = list(range(-SLOTS, 0)), [0] * SLOTS
    for i, key in enumerate(PLAN):
        lent = key[0] == "w" and W_GATE <= key[1] < W_OUT
        s = min(range(SLOTS - 1 if lent else SLOTS), key=lambda j: age[j])
        age[s] = i
        count[s] += 1
        where[key], fills[key], before[key] = s, count[s], last[s]
        last[s] = key
    return where, fills, before


WHERE, FILLS, BEFORE = slots()
LENT = SLOTS - 1
LENT_LAST = max(n for kind, n, *_ in PLAN if kind == "w" and n < W_GATE and WHERE[(kind, n)] == LENT)


def slot_of(key):
    return WHERE[key]


def landed(key):
    return 16 * FILLS[key]


CW = {}


def _columns():
    at = 0
    for name, w in (("ident", 128), ("blockdiag", 128), ("ones", 128), ("half", 2), ("sel9", 9), ("sel8", 8), ("perm", 128),
                    ("negslope", 1), ("pageslope", 8), ("coef1", 1), ("coeflam", 1), ("rowA", 1), ("tri", 16),
                    ("dist", 384), ("distrow", 128), ("maskA", 512), ("maskB", 512)):
        CW[name] = (at, w)
        at += w
    return at


NCONST = _columns()


def slope_of_row(j):
    return 2.0 ** -(j + 1) if j < 8 else 2.0 ** (-2.0 * ((j - 8) // 2 + 1))


def constants():
    c = np.zeros((P, NCONST), np.float32)

    def put(name, a):
        c[:, CW[name][0]:CW[name][0] + CW[name][1]] = a

    p = np.arange(P)
    put("ident", np.eye(P))
    put("blockdiag", p[:, None] // 64 == p[None] // 64)
    put("ones", 1.0)
    put("half", np.stack([p < 64, p >= 64], 1))
    put("sel9", (p[:, None] % 32) == np.arange(9)[None])
    row_s, row_j = p % 32 // 4, 8 * (p % 4 // 2) + 2 * (p // 32) + p % 2
    put("sel8", row_s[:, None] == np.arange(8)[None])
    put("perm", (16 * row_s + row_j)[:, None] == p[None])
    slope = np.array([slope_of_row(j) for j in row_j])
    put("negslope", -slope[:, None])
    put("pageslope", slope[:, None] * 128.0 * np.arange(8)[None])
    isb1 = (row_j >= 8) & (p % 2 == 1)
    put("coef1", (~isb1)[:, None])
    put("coeflam", isb1[:, None])
    put("rowA", (row_j < 8)[:, None])
    n = np.arange(4)
    put("tri", np.broadcast_to((n[None, :] < n[:, None]).reshape(1, 16), (P, 16)))
    k = np.arange(256)
    d0 = np.where(k[None, :128] <= p[:, None], p[:, None] - k[None, :128], BIG)
    d1 = np.where(k[None] <= p[:, None] + 128, p[:, None] + 128 - k[None], BIG)
    put("dist", np.concatenate([d0, d1], 1))
    put("distrow", np.broadcast_to(PAST - np.arange(128)[None], (P, 128)))
    m = p % 32
    col = np.arange(512)
    put("maskA", (col[None] // 64 == m[:, None]))
    put("maskB", (m[:, None] < 8) & (col[None] // 128 == m[:, None] // 2))
    return c


R_BADA, R_N1, R_N2, R_N3, R_QNA, R_KNA, R_QNB, R_KNB, R_SUB, R_LQ, R_LK, NROWS = 0, 72, 80, 88, 96, 97, 98, 99, 100, 101, 102, 103


class Chain:

    def __init__(self, eng, sem):
        self.eng, self.sem, self.base, self.n = eng, sem, 0, 0

    def link(self, ins):
        ins.then_inc(self.sem, 1)
        self.n += 1
        self.eng.wait_ge(self.sem, self.base + self.n)

    def enter(self, i, first, per):
        self.base, self.n, self.per = self.n + (i - first) * per, 0, per
        self.at = self.base

    def leave(self, before, count):
        assert self.n == self.per
        self.base, self.n = 0, before + count * self.per


def build(nc, A, O):
    ctx = ExitStack()
    with ctx:
        at = [((nc.sbuf_base + 31) // 32) * 32]
        end = nc.sbuf_usable_end

        def place(name, shape, dt=F32, where=None):
            size = int(np.prod(shape[1:])) * 4
            where = where if where is not None else at
            h = nc.alloc_sbuf_tensor_at(name, shape, dt, offset=where[0])
            where[0] = (where[0] + size + 31) // 32 * 32
            assert where[0] <= end, (name, where[0], end)
            return h

        def sem(name):
            return ctx.enter_context(nc.semaphore(name))

        const = place("const", [P, NCONST])
        raw_at = [at[0] + 4 * UNIT * s for s in range(SLOTS)]
        raw = [place(f"raw{s}", [P, UNIT]) for s in range(SLOTS)]
        whi = [place(f"whi{s}", [P, UNIT], F32R) for s in range(2)]
        wlo = [place(f"wlo{s}", [P, UNIT], F32R) for s in range(2)]
        x = place("x", [P, KC, T])
        hhi_at = at[0]
        hhi = place("hhi", [P, KC, T], F32R)
        hlo = place("hlo", [P, KC, T], F32R)
        mod = place("mod", [P, NMOD * KC, 9])
        par = place("par", [P, NROWS])
        adarow = place("adarow", [P, 512])
        csilu = place("csilu", [P, KC, 32])
        work_at = at[0]
        work = place("work", [P, KC, T])
        rstd = place("rstd", [P, 2, T])
        misc = place("misc", [P, 64])
        tmps = place("tmps", [P, 2, TS])
        region = at[0]
        r = [region]
        ahi = place("ahi", [P, FC, T], F32R, r)
        alo = place("alo", [P, FC, T], F32R, r)
        sil = place("sil", [P, 2, T], where=r)
        act = place("act", [P, 2, T], where=r)
        yst = place("yst", [P, 2, D], where=r)
        ysts = place("ysts", [TS, D], where=r)
        r = [region]
        xtok = place("xtok", [P, 2, D], where=r)
        xtoks = place("xtoks", [TS, D], where=r)
        rows = place("rows", [NROWS, P], where=r)
        crow = place("crow", [72, P], where=r)
        r = [region]
        kv = [[place(f"kv{a}{s}", [P, 4, 512], where=r) for s in range(KVS - 1)] for a in "AB"]
        kv_lent = [place("kvA_lent", [P, 4, 512], where=[raw_at[LENT]]), place("kvB_lentK", [P, 4, 512], where=[work_at]),
                   place("kvB_lentV", [P, 4, 512], where=[hhi_at])]
        qT = place("qT", [P, KC, T], where=r)
        kT = place("kT", [P, KC, T], where=r)
        vtok = place("vtok", [P, 2, D], where=r)
        vtoks = place("vtoks", [TS, D], where=r)
        gT = place("gT", [P, 2 * KC, T], where=r)
        stat = place("stat", [P, 64], where=r)
        sall_at = r[0]
        sall = place("sall", [P, NPG, RW], where=r)
        area = r[0]
        qpad = [place(f"qpad{s}", [P, KC, 64], where=[sall_at + s * KC * 64 * 4]) for s in range(2)]
        r = [area]
        vT = place("vT", [P, 2, T], where=r)
        kst = place("kst", [P, 2, 256], where=r)
        ksts = place("ksts", [TS, 256], where=r)
        sqb = place("sqb", [P, 2, T], where=r)
        r = [area]
        kTs = [[place(f"kTs{a}{s}", [P, 512], where=r) for s in range(2)] for a in "AB"]
        r = [area]
        prob = place("prob", [P, PAST], where=r)
        b0 = place("b0", [P, P], where=r)
        ecur = place("ecur", [P, P], where=r)
        dcur = place("dcur", [TS, RW], where=r)
        plog = [place(f"plog{h}", [P, 384], where=r) for h in range(2)]
        pts_at = r[0]
        r = [area]
        om = place("om", [P, 2, 512], where=r)
        r = [pts_at]
        pts = [place(f"pts{h}", [P, 384], where=r) for h in range(2)]
        ncur = place("ncur", [P, 1], where=r)
        ev0 = place("ev0", [P, P], where=r)
        r = [area]
        osq = place("osq", [P, 4, T], where=r)

        bank = ctx.enter_context(nc.psum_tensor("bank", [P, 8, 512], F32))

        def C(name, lo=0, hi=None):
            a, w = CW[name]
            return const[:, a + lo:a + (w if hi is None else hi)]

        ident = C("ident")

        s_raw = [sem(f"raw_landed{s}") for s in range(SLOTS)]
        s_rows, s_crow, s_x, s_const = sem("rows_landed"), sem("crow_landed"), sem("x_landed"), sem("const_landed")
        s_hi, s_lo, s_gemm = sem("hi_ready"), sem("lo_ready"), sem("gemm_done")
        s_ada, s_adarow, s_sel, s_mod = sem("ada_multiplied"), sem("adarow_ready"), sem("ada_turned"), sem("mod_ready")
        s_zero = sem("csilu_zeroed")
        s_parT, s_par, s_csilu = sem("params_turned"), sem("params_ready"), sem("csilu_ready")
        s_xT, s_xfirst = sem("x_turned"), sem("x_first")
        s_sq, s_ssum, s_var, s_rstd = sem("squares_ready"), sem("squares_summed"), sem("variance_ready"), sem("rstd_ready")
        s_ohi, s_olo, s_turned_g = sem("ohi_ready"), sem("olo_ready"), sem("gated_moba")
        s_h, s_hhi, s_hlo = sem("h_ready"), sem("hhi_ready"), sem("hlo_ready")
        s_sil, s_act, s_ahi, s_alo = sem("silu_ready"), sem("act_ready"), sem("ahi_ready"), sem("alo_ready")
        s_xup = sem("x_updated")
        s_coef = sem("coefficients_ready")
        s_lamsum, s_lamexp = sem("lambda_sums"), sem("lambda_exp")
        s_proj, s_nsum, s_nvar, s_nrstd, s_qk = sem("proj_out"), sem("head_squares_summed"), sem("head_variance"), sem("head_rstd"), sem("qk_ready")
        s_turn, s_tok, s_rowout = sem("kv_turned"), sem("kv_tokens_ready"), sem("kv_rows_stored")
        s_qpad, s_kTp = sem("q_padded"), [sem(f"k_turned{a}") for a in "AB"]
        s_kv = [[sem(f"kv_landed{a}{s}") for s in range(KVS)] for a in "AB"]
        s_kTs, s_kS = [sem(f"k_turned_ready{a}") for a in "AB"], [sem(f"k_scored{a}") for a in "AB"]
        s_ncur = sem("own_scores_ready")
        s_sig, s_sigend = sem("gate_out"), sem("last_gates_ready")
        s_ecur, s_cur = sem("current_products"), sem("current_scores")
        s_logit, s_prob, s_pscaled, s_diag = sem("logits_ready"), sem("probs_ready"), sem("probs_scaled"), sem("diag_ready")
        s_dps, s_dcur = sem("current_weights_psum"), sem("current_weights_ready")
        s_pT, s_pTs = sem("probs_turned"), sem("probs_turned_ready")
        s_pv, s_pvd, s_om, s_ext = sem("v_used"), sem("sample_out"), sem("sample_masked"), sem("sample_extracted")
        s_psc, s_plog, s_pexp, s_pscale = sem("prompt_scores"), sem("prompt_logits"), sem("prompt_exp"), sem("prompt_probs")
        s_ppT, s_pps, s_po, s_pout = sem("prompt_probs_turned"), sem("prompt_probs_ready"), sem("prompt_out"), sem("prompt_out_ready")
        s_samp = sem("sample_out_ready")
        s_osq, s_osum, s_ovar, s_orstd, s_o = sem("o_squares"), sem("o_summed"), sem("o_variance"), sem("o_rstd"), sem("o_ready")
        s_mix = sem("mix_ready")
        s_yT, s_ys, s_yout = sem("y_turned"), sem("y_staged"), sem("y_stored")
        s_vch, s_ach = sem("vector_steps"), sem("scalar_steps")

        block = ctx.enter_context(nc.Block())

        gate_w = (A["ffn1_w_gate"], A["ffn2_w_gate"])
        up_w = (A["ffn1_w_up"], A["ffn2_w_up"])
        down_w = (A["ffn1_w_down"], A["ffn2_w_down"])

        def km(w):
            return w[0].rearrange("(k p) n -> p k n", p=P)

        def ff_block(w, i):
            return km(w)[:, :, bass.ds(i * 256, 256)]

        def fixed_block(n):
            for first, w in ((W_DN1, down_w[0]), (W_DN2, down_w[1])):
                if first <= n < first + 12:
                    cb, third = divmod(n - first, 3)
                    k1 = min(FC, 8 * third + 8)
                    return km(w)[:, 8 * third:k1, cb * 256:cb * 256 + 256], k1 - 8 * third, 256
            if W_QKV <= n < W_BR:
                c = (n - W_QKV) * 256
                return km(A["w_in"])[:, :, c:c + 256], KC, 256
            if W_BR <= n < W_OUT:
                w = A["w_branch_diff"] if n >= W_BR + 2 else A["w_branch_moba"]
                c = (n - W_BR) % 2 * 512
                return km(w)[:, :, c:c + 512], 4, 512
            c = (n - W_OUT) * 256
            return km(A["w_out"])[:, :, c:c + 256], KC, 256

        def half_view(tensor, key, t):
            n = key[1]
            nk, w = (KC, 256) if W_FF1 <= n < W_DN1 or W_FF2 <= n < W_DN2 else fixed_block(n)[1:]
            return tensor[:, 0:nk * w].rearrange("p (k n) -> p k n", k=nk)[:, :, t * w // 2:(t + 1) * w // 2]

        def half_done(n, t):
            return 2 * n + t + 1

        CACHE_K = (A["cache_k_moba"][0].rearrange("n t h d -> n t (h d)"), A["cache_k_diff"][0].rearrange("n t h d -> n t (h d)"))
        CACHE_V = (A["cache_v_moba"][0].rearrange("n t h d -> n t (h d)"), A["cache_v_diff"][0].rearrange("n t h d -> n t (h d)"))

        def kv_slot(ab, use):
            if use % KVS < KVS - 1:
                return kv[ab][use % KVS]
            return kv_lent[0 if ab == 0 else 1 if use < 16 else 2]

        def load_half(eng, ab, cache, s, half, use):
            for q in range(4):
                g = 4 * half + q
                page = eng.value_load(A["page_table"][s:s + 1, g:g + 1], min_val=0, max_val=NPHYS - 1)
                eng.dma_start(kv_slot(ab, use)[:, q, :], cache[bass.ds(page, 1)].rearrange("a t d -> (a t) d")).then_inc(s_kv[ab][use % KVS], 16)

        def kv_landed(use):
            return 64 * (use // KVS + 1)

        def kv_load(eng, ab, use):
            s, half = divmod(use % 16, 2)
            prev = use - KVS
            if use == KVS - 1:
                if ab == 0:
                    eng.wait_ge(s_lo, half_done(LENT_LAST, 1))
                else:
                    eng.wait_ge(s_ecur, 1)
            if ab == 1 and use >= 16 and use % KVS == KVS - 1 and use - KVS < 16:
                eng.wait_ge(s_gemm, half_done(W_GATE + 7, 1))
            if 0 <= prev < 16:
                eng.wait_ge(s_kTs[ab], 4 * prev + 4)
            elif prev >= 16:
                eng.wait_ge(s_pv, 2 * (prev - 16) + ab + 1)
            load_half(eng, ab, (CACHE_K if use < 16 else CACHE_V)[ab], s, half, use)

        def chunk_of(ab, g):
            return (g + 2 * ab) % 4

        def turned_chunk(eng, ab, s, g, copy):
            eng.wait_ge(s_kTp[ab], NPG * s + g + 1)
            if NPG * s + g >= 2:
                eng.wait_ge(s_kS[ab], NPG * s + g - 1)
            copy(kTs[ab][g % 2][:, :], bank[:, 2 + 2 * (g % 2) + ab, :]).then_inc(s_kTs[ab], 1)

        def gate(eng, s, func):
            eng.wait_ge(s_gemm, half_done(W_GATE + s, 1))
            b = 2 if s == 7 else 0
            nc.scalar.activation(gT[:, 2 * s:2 * s + 2, :], bank[:, b:b + 2, 0:T], func).then_inc(s_sig, 1)

        @block.sync
        def _(sp):
            def slot_free(key, shift=0):
                prev = BEFORE[key]
                if prev is None:
                    return
                if slot_of(key) == LENT and key[0] == "w" and prev[0] == "w" and prev[1] < W_GATE <= key[1]:
                    sp.wait_ge(s_pv, 2 * (4 * TS - 1 - (4 * TS - 1 - (KVS - 1)) % KVS - 16) + 1)
                if prev[0] == "ada":
                    sp.wait_ge(s_ada, prev[1] + 1 + shift)
                else:
                    sp.wait_ge(s_lo, half_done(prev[1], 1) + 2 * shift)

            def load_ada(c, half, key, shift=0):
                slot_free(key, shift)
                src = A["w_ada"][0].rearrange("(k p) n -> p k n", p=P)[:, 4 * half:4 * half + 4, bass.ds(c * 512, 512)]
                s = slot_of(key)
                sp.dma_start(raw[s][:, :].rearrange("p (k n) -> p k n", k=4), src).then_inc(s_raw[s], 16)

            def load_w(n):
                src, nk, w = fixed_block(n)
                slot_free(("w", n))
                s = slot_of(("w", n))
                sp.dma_start(raw[s][:, 0:nk * w].rearrange("p (k n) -> p k n", k=nk), src).then_inc(s_raw[s], 16)

            def load_ff(w, i, key, shift=0):
                slot_free(key, shift)
                s = slot_of(key)
                sp.dma_start(raw[s][:, :].rearrange("p (k n) -> p k n", k=KC), ff_block(w, i)).then_inc(s_raw[s], 16)

            for c in range(ADA_PRO):
                for half in range(2):
                    load_ada(c, half, ("ada", c, half))

            def ff1_step(i, first, rate):
                d = i - first if rate else 0
                load_ff(gate_w[0], i, ("w", W_FF1 + 2 * first), 2 * d)
                load_ada(ADA_PRO + i, 0, ("ada", ADA_PRO + first, 0), d)
                load_ada(ADA_PRO + i, 1, ("ada", ADA_PRO + first, 1), d)
                load_ff(up_w[0], i, ("w", W_FF1 + 2 * first + 1), 2 * d)

            ff1_step(0, 0, 0)
            with sp.Fori(1, NPAIR) as i:
                ff1_step(i, 1, 1)
            for i in range(3):
                for u in range(4):
                    load_w(W_DN1 + 4 * i + u)
                c = ADA_PRO + NPAIR + i
                for half in range(2):
                    load_ada(c, half, ("ada", c, half))
            for u in range(6):
                load_w(W_QKV + u)
            sp.wait_ge(s_gemm, half_done(W_QKV - 1, 1))
            for use in range(KVS - 1):
                kv_load(sp, 0, use)
            for u in range(6, 12):
                load_w(W_QKV + u)
            for n in range(W_GATE, W_GATE + 3):
                load_w(n)
            kv_load(sp, 0, KVS - 1)
            for s in range(TS):
                load_w(W_GATE + 3 + s)
                kv_load(sp, 0, 2 * s + KVS)
                kv_load(sp, 0, 2 * s + KVS + 1)
            for use in range(2 * TS + KVS, 4 * TS):
                kv_load(sp, 0, use)
                if use == 2 * TS + KVS:
                    load_w(W_BR + 3)
            for n in range(W_OUT, W_FF2):
                load_w(n)

            def ff2_pair(i, key_pair, d):
                load_ff(gate_w[1], i, ("w", W_FF2 + 2 * key_pair), 2 * d)
                load_ff(up_w[1], i, ("w", W_FF2 + 2 * key_pair + 1), 2 * d)

            ff2_pair(0, 0, 0)
            ff2_pair(1, 1, 0)
            with sp.Fori(1, NPAIR // 2) as i:
                ff2_pair(2 * i, 2, 2 * (i - 1))
                ff2_pair(2 * i + 1, 3, 2 * (i - 1))
            ff2_pair(NPAIR - 1, NPAIR - 1, 0)
            for u in range(12):
                load_w(W_DN2 + u)
            for cb in range(4):
                sp.wait_ge(s_ys, 2 * (cb + 1))
                sp.dma_start(O["y_prompt"][0].rearrange("(a p) d -> p a d", p=P)[:, :, cb * 256:cb * 256 + 256],
                             yst[:, :, cb * 256:cb * 256 + 256]).then_inc(s_yout, 16)
                sp.dma_start(O["y_sample"][:, 0, cb * 256:cb * 256 + 256], ysts[:, cb * 256:cb * 256 + 256]).then_inc(s_yout, 16)
            sp.wait_ge(s_yout, 16 * 8)
            sp.wait_ge(s_rowout, 16 * 16)

        @block.gpsimd
        def _(pool):
            pool.dma_start(const[:, :], A["consts"]).then_inc(s_const, 16)
            pool.wait_ge(s_gemm, half_done(W_QKV - 1, 1))
            for use in range(KVS - 1):
                kv_load(pool, 1, use)
            turned = 0
            for u in range(12):
                ab, kind, p = u // 6, u % 6 // 2, u % 2
                if kind == 0:
                    continue
                turned += 1
                pool.wait_ge(s_tok, 2 * turned)
                c0 = 256 * p
                name = ("k", "v")[kind - 1] + ("_moba", "_diff")[ab]
                dst = O[name + "_prompt"][0, 0].rearrange("(a p) h d -> p a (h d)", p=P)[:, :, c0:c0 + 256]
                dsts = O[name + "_sample"][0, :, 0].rearrange("s h d -> s (h d)")[:, c0:c0 + 256]
                f0 = 512 * ab + c0
                src = kst[:, :, :] if kind == 1 else vtok[:, :, f0:f0 + 256]
                srcs = ksts[:, :] if kind == 1 else vtoks[:, f0:f0 + 256]
                pool.dma_start(dst, src).then_inc(s_rowout, 16)
                pool.dma_start(dsts, srcs).then_inc(s_rowout, 16)
            for use in range(KVS - 1, 4 * TS):
                kv_load(pool, 1, use)

        @block.scalar
        def _(a):
            a.dma_start(rows[:, :], A["params"]).then_inc(s_rows, 16)
            a.dma_start(crow[:, :], A["c_rows"]).then_inc(s_crow, 16)
            a.dma_start(xtok[:, :, :], A["x_prompt"][0].rearrange("(a p) d -> p a d", p=P)).then_inc(s_x, 16)
            a.dma_start(xtoks[:, :], A["x_sample"][:, 0, :]).then_inc(s_x, 16)

            def hi(n, t, key=None, d=0):
                key = key or ("w", n)
                s = slot_of(key)
                a.wait_ge(s_raw[s], landed(key) + 16 * d)
                if not (isinstance(n, int) and n < 2):
                    recut = isinstance(n, int) and n in (W_BR, W_BR + 1, W_OUT, W_OUT + 1)
                    a.wait_ge(s_gemm, half_done(n, 1 if recut else t) - 4)
                nc.scalar.activation(half_view(whi[key[1] % 2], key, t), half_view(raw[s], key, t), ACT.Copy).then_inc(s_hi, 1)

            def ada_row(c):
                a.wait_ge(s_ada, c + 1)
                if not (isinstance(c, int) and c == 0):
                    a.wait_ge(s_sel, c)
                nc.scalar.activation(adarow[:, :], bank[:, 4, :], ACT.Copy).then_inc(s_adarow, 1)

            def squares(cb, ready, count):
                a.wait_ge(ready, count)
                nc.scalar.activation(work[:, 2 * cb:2 * cb + 2, :], x[:, 2 * cb:2 * cb + 2, :], ACT.Square).then_inc(s_sq, 1)

            def root(ap, ready, count, done):
                a.wait_ge(ready, count)
                nc.scalar.activation(ap, ap, ACT.Sqrt).then_inc(done, 1)

            def norm_hi(t):
                sh = 3 * t * KC
                for c in range(KC):
                    a.wait_ge(s_h, KC * t + c + 1)
                    nc.scalar.activation(hhi[:, c, 0:TP], work[:, c, 0:TP], ACT.Identity, bias=mod[:, sh + c, 0:1]).then_inc(s_hhi, 1)

            def silu(i, base, pairs):
                a.wait_ge(s_gemm, half_done(base + 2 * i, 1))
                if not (isinstance(i, int) and i + pairs == 0):
                    a.wait_ge(s_act, pairs + i)
                nc.scalar.activation(sil[:, :, :], bank[:, 0:2, 0:T], ACT.Silu).then_inc(s_sil, 1)

            def act_hi(i, pairs):
                a.wait_ge(s_act, pairs + i + 1)
                nc.scalar.activation(ahi[:, bass.ds(2 * i, 2), :], act[:, :, :], ACT.Copy).then_inc(s_ahi, 1)

            def ff_turn(i, base, pairs, key_i, d, ada):
                k = lambda u: ("w", base + 2 * key_i + u)
                hi(base + 2 * i + 1, 1, k(1), d)
                silu(i, base, pairs)
                if ada:
                    ada_row(ADA_PRO + i)
                hi(base + 2 * i + 2, 0, k(2), d)
                hi(base + 2 * i + 2, 1, k(2), d)
                hi(base + 2 * i + 3, 0, k(3), d)
                act_hi(i, pairs)

            a.wait_ge(s_parT, 1)
            a.wait_ge(s_zero, 1)
            nc.scalar.activation(csilu[:, :, 0:9], bank[:, 6, 0:72].rearrange("p (k m) -> p k m", k=KC), ACT.Silu).then_inc(s_csilu, 1)
            a.wait_ge(s_lamsum, 1)
            nc.scalar.activation(misc[:, 4:6], bank[:, 6, 0:2], ACT.Exp).then_inc(s_lamexp, 1)
            for cb in range(4):
                squares(cb, s_xfirst, cb // 2 + 1)
            for c in range(ADA_PRO):
                ada_row(c)
                if c == 0:
                    root(rstd[:, 0, :], s_var, 1, s_rstd)
            hi(W_FF1, 0)
            hi(W_FF1, 1)
            norm_hi(0)
            hi(W_FF1 + 1, 0)
            ff_turn(0, W_FF1, 0, 0, 0, True)
            with a.Fori(1, NPAIR - 1) as i:
                ff_turn(i, W_FF1, 0, 1, i - 1, True)
            ff_turn(NPAIR - 1, W_FF1, 0, NPAIR - 1, 0, True)

            def y_out(cb):
                a.wait_ge(s_yT, cb + 1)
                nc.scalar.activation(yst[:, :, cb * 256:cb * 256 + 256], bank[:, 4, :].rearrange("p (a n) -> p a n", a=2), ACT.Copy).then_inc(s_ys, 1)
                nc.scalar.activation(ysts[:, cb * 256:cb * 256 + 256], bank[0:TS, 5, 0:256], ACT.Copy).then_inc(s_ys, 1)

            def down(first, ada):
                for m in range(3, 27 if ada else 24):
                    if ada and m in (12, 20):
                        ada_row(ADA_PRO + NPAIR + (m - 12) // 8)
                    if not ada and m in (14, 20):
                        y_out((m - 14) // 6)
                    if ada and m in (11, 17, 23):
                        squares((m - 11) // 6, s_xup, (m - 11) // 6 + 1)
                    hi(first + m // 2, m % 2)

            down(W_DN1, True)
            squares(3, s_xup, 4)
            root(rstd[:, 0, :], s_var, 2, s_rstd)
            ada_row(ADAC - 1)
            norm_hi(1)

            nsq = toks = 0
            for u in range(12):
                n = W_QKV + u
                ab, kind, p = u // 6, u % 6 // 2, u % 2
                hi(n + 1, 1)
                hi(n + 2, 0)
                if u and (u - 1) % 6 < 4:
                    root(rstd[:, :, :], s_nvar, nsq, s_nrstd)
                b = 2 * (u % 2)
                c0 = 4 * ab + 2 * p
                a.wait_ge(s_gemm, half_done(n, 1))
                src = bank[:, b:b + 2, 0:T]
                if kind < 2:
                    dst = (qT, kT)[kind]
                    nc.scalar.activation(dst[:, c0:c0 + 2, :], src, ACT.Copy)
                    if nsq:
                        a.wait_ge(s_nsum, nsq)
                    nc.scalar.activation(sqb[:, :, :], src, ACT.Square).then_inc(s_proj, 1)
                    nsq += 1
                else:
                    if toks:
                        a.wait_ge(s_turn, toks)
                    nc.scalar.activation(vT[:, :, :], src, ACT.Copy).then_inc(s_proj, 1)
                if kind > 0:
                    toks += 1

            for s in range(TS):
                if s == 0:
                    a.wait_ge(s_rowout, 16 * 16)
                    a.wait_ge(s_turn, 8)
                elif s <= 6:
                    gate(a, s - 1, ACT.Sigmoid)
                for g in range(NPG):
                    turned_chunk(a, 0, s, g, lambda out, in_: nc.scalar.activation(out, in_, ACT.Copy))
                if s < 6:
                    hi(W_GATE + s + 1, 1)
                    hi(W_GATE + s + 2, 0)
                if s == 6:
                    hi(W_GATE + 7, 1)
            hi(W_BR, 0)
            hi(W_BR, 1)
            gate(a, 6, ACT.Copy)
            hi(W_BR + 1, 0)
            hi(W_BR + 1, 1)
            gate(a, 7, ACT.Copy)
            a.wait_ge(s_logit, 1)
            nc.scalar.activation(prob[:, :], prob[:, :], ACT.Exp, bias=stat[:, 3:4], accum_out=stat[:, 4:5])
            nc.scalar.activation(stat[:, 5:6], ncur[:, :], ACT.Exp, bias=stat[:, 3:4]).then_inc(s_prob, 1)

            def prompt_exp(c):
                for h in range(2):
                    a.wait_ge(s_plog, 2 * c + h + 1)
                    o = 16 * h + 16
                    nc.scalar.activation(plog[h][:, 0:128], plog[h][:, 0:128], ACT.Exp, bias=stat[:, o + 3:o + 4], accum_out=stat[:, o + 5:o + 6])
                    nc.scalar.activation(plog[h][:, 128:384], plog[h][:, 128:384], ACT.Exp, bias=stat[:, o + 4:o + 5],
                                         accum_out=stat[:, o + 6:o + 7]).then_inc(s_pexp, 1)

            a.wait_ge(s_pT, 1)
            nc.scalar.activation(sall[:, :, 0:P], bank[:, 6:8, :].rearrange("p a (g r) -> p (a g) r", g=4), ACT.Copy).then_inc(s_pTs, 1)
            a.wait_ge(s_dps, 1)
            nc.scalar.activation(dcur[:, 0:P], bank[0:TS, 3, 0:P], ACT.Copy).then_inc(s_dcur, 1)
            npp = 0
            prompt_exp(0)
            for c in range(KC):
                for h in range(2 if c < 4 else 1):
                    npp += 1
                    a.wait_ge(s_ppT, npp)
                    if c:
                        a.wait_ge(s_po, c)
                    nc.scalar.activation(pts[h][:, :], bank[:, 6 + h, 0:384], ACT.Copy).then_inc(s_pps, 1)
                if c + 1 < KC:
                    prompt_exp(c + 1)
                a.wait_ge(s_po, c + 1)
                nc.scalar.activation(work[:, c, 0:TP], bank[:, 2, 0:TP], ACT.Copy).then_inc(s_pout, 1)
            a.wait_ge(s_samp, 1)
            a.wait_ge(s_pout, KC)
            nc.scalar.activation(osq[:, :, :], work[:, 4:8, :], ACT.Square).then_inc(s_osq, 1)
            nc.scalar.activation(hhi[:, 0:4, :], work[:, 0:4, :], ACT.Copy).then_inc(s_ohi, 1)
            nc.scalar.activation(gT[:, 12:16, :], gT[:, 12:16, :], ACT.Sigmoid).then_inc(s_sigend, 1)
            root(osq[:, :, :], s_ovar, 1, s_orstd)
            a.wait_ge(s_o, 1)
            nc.scalar.activation(hhi[:, 4:8, :], work[:, 4:8, :], ACT.Copy).then_inc(s_ohi, 1)
            for m in range(4, 10):
                hi(W_BR + m // 2, m % 2)
            a.wait_ge(s_mix, 1)
            nc.scalar.activation(ahi[:, 0:4, :], gT[:, 0:4, :], ACT.Copy).then_inc(s_ahi, 1)
            hi(W_OUT + 1, 0)
            hi(W_OUT + 1, 1)
            a.wait_ge(s_mix, 2)
            nc.scalar.activation(ahi[:, 4:8, :], gT[:, 4:8, :], ACT.Copy).then_inc(s_ahi, 1)
            for m in range(4, 11):
                if m in (6, 8, 10):
                    squares((m - 6) // 2, s_xup, 5 + (m - 6) // 2)
                hi(W_OUT + m // 2, m % 2)
            squares(3, s_xup, 8)
            root(rstd[:, 0, :], s_var, 3, s_rstd)
            nc.scalar.activation(misc[:, 20:21], misc[:, 21:22], ACT.Silu)
            norm_hi(2)
            with a.Fori(0, NPAIR // 2) as i:
                ff_turn(2 * i, W_FF2, NPAIR, 0, i, False)
                ff_turn(2 * i + 1, W_FF2, NPAIR, 1, i, False)
            ff_turn(NPAIR - 1, W_FF2, NPAIR, NPAIR - 1, 0, False)
            down(W_DN2, False)
            y_out(2)
            y_out(3)

        @block.vector
        def _(v):
            ch = Chain(v, s_vch)
            dve = nc.vector

            def lo(n, t, key=None, d=0):
                key = key or ("w", n)
                s = slot_of(key)
                v.wait_ge(s_raw[s], landed(key) + 16 * d)
                v.wait_ge(s_hi, half_done(n, t))
                dve.tensor_tensor(half_view(wlo[key[1] % 2], key, t), half_view(raw[s], key, t), half_view(whi[key[1] % 2], key, t).bitcast(F32),
                                  ALU.subtract).then_inc(s_lo, 1)

            def mod_add(c):
                v.wait_ge(s_sel, c + 1)
                b = par[:, bass.ds(R_BADA + 4 * c, 4)].unsqueeze(2).broadcast_to([P, 4, 9])
                dve.tensor_tensor(mod[:, bass.ds(4 * c, 4), :], bank[:, 5, 0:36].rearrange("p (t m) -> p t m", t=4), b, ALU.add).then_inc(s_mod, 1)

            def coefficients(t, row):
                m0 = (3 * t + 1) * KC
                gain = par[:, row:row + KC].unsqueeze(2).broadcast_to([P, KC, 9])
                ch.link(dve.scalar_tensor_tensor(out=mod[:, m0:m0 + KC, :], in0=mod[:, m0:m0 + KC, :], scalar=1.0, in1=gain, op0=ALU.add, op1=ALU.mult))

            def variance(t):
                v.wait_ge(s_ssum, t + 1)
                ch.link(dve.tensor_scalar(rstd[:, 0, :], bank[:, 6, 0:T], 1.0 / D, EPS, ALU.mult, ALU.add))
                dve.reciprocal(rstd[:, 0, :], rstd[:, 0, :]).then_inc(s_var, 1)

            def norm_rows(t):
                v.wait_ge(s_rstd, t + 1)
                sh, sc = 3 * t * KC, (3 * t + 1) * KC
                ws = work[:, :, TP:T]
                ch.link(dve.tensor_tensor(ws, x[:, :, TP:T], rstd[:, 0:1, TP:T].broadcast_to([P, KC, TS]), ALU.mult))
                ch.link(dve.tensor_tensor(ws, ws, mod[:, sc:sc + KC, 1:9], ALU.mult))
                ch.link(dve.tensor_tensor(ws, ws, mod[:, sh:sh + KC, 1:9], ALU.add))
                ch.link(dve.tensor_copy(hhi[:, :, TP:T], ws))
                ch.link(dve.tensor_tensor(hlo[:, :, TP:T], ws, hhi[:, :, TP:T].bitcast(F32), ALU.subtract))

                def scaled(c):
                    dve.scalar_tensor_tensor(out=work[:, c, 0:TP], in0=x[:, c, 0:TP], scalar=mod[:, sc + c, 0:1], in1=rstd[:, 0, 0:TP],
                                             op0=ALU.mult, op1=ALU.mult).then_inc(s_h, 1)

                scaled(0)
                for c in range(KC):
                    if c + 1 < KC:
                        scaled(c + 1)
                    v.wait_ge(s_h, KC * t + c + 1)
                    v.wait_ge(s_hhi, KC * t + c + 1)
                    dve.scalar_tensor_tensor(out=hlo[:, c, 0:TP], in0=work[:, c, 0:TP], scalar=mod[:, sh + c, 0:1], in1=hhi[:, c, 0:TP].bitcast(F32),
                                             op0=ALU.add, op1=ALU.subtract).then_inc(s_hlo, 1)

            def act_mul(i, base, pairs):
                v.wait_ge(s_sil, pairs + i + 1)
                v.wait_ge(s_gemm, half_done(base + 2 * i + 1, 1))
                dve.tensor_tensor(act[:, :, :], sil[:, :, :], bank[:, 2:4, 0:T], ALU.mult).then_inc(s_act, 1)

            def act_lo(i, ahis):
                v.wait_ge(s_ahi, ahis + i + 1)
                dve.tensor_tensor(alo[:, bass.ds(2 * i, 2), :], act[:, :, :], ahi[:, bass.ds(2 * i, 2), :].bitcast(F32), ALU.subtract).then_inc(s_alo, 1)

            def ff_turn(i, base, pairs, ahis, key_i, d, ada):
                k = lambda u: ("w", base + 2 * key_i + u)
                lo(base + 2 * i + 1, 1, k(1), d)
                lo(base + 2 * i + 2, 0, k(2), d)
                lo(base + 2 * i + 2, 1, k(2), d)
                lo(base + 2 * i + 3, 0, k(3), d)
                act_mul(i, base, pairs)
                act_lo(i, ahis)
                if ada:
                    mod_add(ADA_PRO + i)

            def x_update(b, m0, gate):
                g = gate * KC + m0
                if x_update.n:
                    v.wait_ge(s_xup, x_update.n)
                x_update.n += 1
                for t in range(2):
                    dve.scalar_tensor_tensor(out=x[:, m0 + t, 0:TP], in0=bank[:, b + t, 0:TP], scalar=mod[:, g + t, 0:1], in1=x[:, m0 + t, 0:TP],
                                             op0=ALU.mult, op1=ALU.add)
                ch.link(dve.tensor_tensor(tmps[:, :, :], bank[:, b:b + 2, TP:T], mod[:, g:g + 2, 1:9], ALU.mult))
                dve.tensor_tensor(x[:, m0:m0 + 2, TP:T], x[:, m0:m0 + 2, TP:T], tmps[:, :, :], ALU.add).then_inc(s_xup, 1)

            x_update.n = 0
            ch.link(dve.memset(csilu[:, :, :], 0.0))
            dve.memset(misc[:, :], 0.0).then_inc(s_zero, 1)
            v.wait_ge(s_parT, 1)
            dve.tensor_copy(par[:, :], bank[:, 7, 0:NROWS]).then_inc(s_par, 1)
            v.wait_ge(s_par, 1)
            v.wait_ge(s_const, 16)
            v.wait_ge(s_zero, 1)
            ch.link(dve.tensor_tensor(misc[:, 0:1], par[:, R_LQ:R_LQ + 1], par[:, R_LK:R_LK + 1], ALU.mult))
            dve.tensor_scalar(misc[:, 2:4], C("half"), misc[:, 0:1], None, ALU.mult).then_inc(s_par, 1)
            ch.link(dve.tensor_scalar(misc[:, 8:9], par[:, R_QNA:R_QNA + 1], 0.125, None, ALU.mult))
            ch.link(dve.tensor_scalar(misc[:, 9:10], par[:, R_QNB:R_QNB + 1], 0.125, None, ALU.mult))
            ch.link(dve.tensor_copy(misc[:, 10:11], par[:, R_KNA:R_KNA + 1]))
            ch.link(dve.tensor_copy(misc[:, 11:12], par[:, R_KNB:R_KNB + 1]))
            ch.link(dve.tensor_scalar(misc[:, 12:13], par[:, R_SUB:R_SUB + 1], 1.0 - LAM_INIT, None, ALU.mult))
            for r2 in range(2):
                v.wait_ge(s_xT, r2 + 1)
                dve.tensor_copy(x[:, 4 * r2:4 * r2 + 4, :], bank[:, 0:4, 0:T]).then_inc(s_xfirst, 1)
            v.wait_ge(s_lamexp, 1)
            ch.link(dve.tensor_tensor(misc[:, 6:7], misc[:, 5:6], misc[:, 4:5], ALU.subtract))
            ch.link(dve.tensor_scalar(misc[:, 6:7], misc[:, 6:7], -LAM_INIT, None, ALU.add))
            ch.link(dve.tensor_scalar(misc[:, 7:8], C("coeflam"), misc[:, 6:7], C("coef1"), ALU.mult, ALU.add))
            variance(0)
            for c in range(ADA_PRO):
                mod_add(c)
            v.wait_ge(s_mod, ADA_PRO)
            coefficients(0, R_N1)
            lo(W_FF1, 0)
            lo(W_FF1, 1)
            norm_rows(0)
            lo(W_FF1 + 1, 0)
            ff_turn(0, W_FF1, 0, 0, 0, 0, True)
            with v.Fori(1, NPAIR - 1) as i:
                ff_turn(i, W_FF1, 0, 0, 1, i - 1, True)
            ff_turn(NPAIR - 1, W_FF1, 0, 0, NPAIR - 1, 0, True)

            def down(first, gate, ada):
                for m in range(3, 27 if ada else 24):
                    if ada and m == 4:
                        v.wait_ge(s_mod, 6)
                        ch.link(dve.tensor_scalar(mod[:, 2 * KC:3 * KC, :], mod[:, 2 * KC:3 * KC, :], 0.5, None, ALU.mult))
                        v.wait_ge(s_mod, 10)
                        coefficients(1, R_N2)
                    if m in (10, 16, 22):
                        cb = (m - 10) // 6
                        v.wait_ge(s_gemm, half_done(first + 3 * cb + 2, 1))
                        x_update(2 * (cb % 2), 2 * cb, gate)
                    if ada and m in (15, 23):
                        mod_add(ADA_PRO + NPAIR + (m - 15) // 8)
                    lo(first + m // 2, m % 2)
                v.wait_ge(s_gemm, half_done(first + 11, 1))
                x_update(2, 6, gate)

            down(W_DN1, 2, True)
            variance(1)
            norm_rows(1)
            mod_add(ADAC - 1)

            nk = tk = 0

            def head_variance(u):
                v.wait_ge(s_nsum, nk)
                if nk > 1:
                    v.wait_ge(s_qk, nk - 1)
                ch.link(dve.tensor_scalar(rstd[:, :, :], bank[:, 6:8, 0:T], 1.0 / 64, EPS, ALU.mult, ALU.add))
                dve.reciprocal(rstd[:, :, :], rstd[:, :, :]).then_inc(s_nvar, 1)

            def head_norm(u):
                ab, kind, p = u // 6, u % 6 // 2, u % 2
                v.wait_ge(s_nrstd, nk)
                dst = (qT, kT)[kind][:, 4 * ab + 2 * p:4 * ab + 2 * p + 2, :]
                g = 8 + 2 * kind + ab
                dve.scalar_tensor_tensor(out=dst, in0=dst, scalar=misc[:, g:g + 1], in1=rstd[:, :, :], op0=ALU.mult, op1=ALU.mult).then_inc(s_qk, 1)

            def tokens(u):
                ab, kind, p = u // 6, u % 6 // 2, u % 2
                v.wait_ge(s_turn, tk)
                f0 = 512 * ab + 256 * p
                if kind == 1 and tk > 1:
                    v.wait_ge(s_rowout, 32 * (tk - 1))
                dst = kst[:, :, :] if kind == 1 else vtok[:, :, f0:f0 + 256]
                dsts = ksts[:, :] if kind == 1 else vtoks[:, f0:f0 + 256]
                dve.tensor_copy(dst, bank[:, 4, :].rearrange("p (a n) -> p a n", a=2)).then_inc(s_tok, 1)
                dve.tensor_copy(dsts, bank[0:TS, 5, 0:256]).then_inc(s_tok, 1)

            for u in range(13):
                if u < 12:
                    lo(W_QKV + u + 1, 1)
                w = (u - 1) % 6 // 2
                if u > 0 and w < 2:
                    nk += 1
                    head_variance(u - 1)
                if u < 12:
                    lo(W_QKV + u + 2, 0)
                if u > 0 and w < 2:
                    head_norm(u - 1)
                if u > 0 and w > 0:
                    tk += 1
                    tokens(u - 1)
            v.wait_ge(s_qk, 8)
            for buf in range(2):
                ins = dve.memset(qpad[buf][:, :, :], 0.0)
            ch.link(ins)

            def pad_q(s):
                if s >= 2:
                    for ab in range(2):
                        v.wait_ge(s_kS[ab], NPG * (s - 1))
                for h in range(2):
                    ins = dve.tensor_scalar(qpad[s % 2][:, :, 30 + h], qT[:, :, TP + s], C("half", h, h + 1), None, ALU.mult)
                ins.then_inc(s_qpad, 1)

            pad_q(0)
            pad_q(1)
            v.wait_ge(s_turn, 8)
            prod = work[:, 0, 0:64].rearrange("p (c s) -> p c s", c=KC)
            ch.link(dve.tensor_tensor(prod, qT[:, :, TP:T], kT[:, :, TP:T], ALU.mult))
            for ab in range(2):
                for h in range(2):
                    ins = dve.tensor_scalar(ev0[:, :].rearrange("p (m s a h) -> p m s a h", m=4, s=TS, a=2)[:, :, :, ab, h], prod[:, 4 * ab:4 * ab + 4, :],
                                            C("half", h, h + 1), None, ALU.mult)
            ins.then_inc(s_ecur, 1)
            v.wait_ge(s_mod, ADAC)
            coefficients(2, R_N3)
            ch.link(dve.tensor_scalar(mod[:, 8 * KC:9 * KC, :], mod[:, 8 * KC:9 * KC, :], 0.5, None, ALU.mult))
            v.wait_ge(s_cur, 1)
            dve.tensor_copy(ncur[:, :], bank[:, 7, 0:1]).then_inc(s_ncur, 1)

            v.wait_ge(s_rowout, 16 * 16)
            for s in range(TS):
                for g in range(NPG):
                    turned_chunk(v, 1, s, g, dve.tensor_copy)
                    if g == 2 and 1 <= s < TS - 1:
                        pad_q(s + 1)
                if s < 6:
                    lo(W_GATE + s + 1, 1)
                    lo(W_GATE + s + 2, 0)
                if s == 6:
                    lo(W_GATE + 7, 1)

            for ab in range(2):
                v.wait_ge(s_kS[ab], NPG * TS)
            ch.link(dve.tensor_scalar(b0[:, :], C("distrow"), C("negslope"), None, ALU.mult))
            blk = stat[:, 8:12]
            ch.link(dve.tensor_reduce(blk, bank[:, 6:8, :].rearrange("p a (b n) -> p (a b) n", n=256), AX.X, ALU.add))
            bm = blk.unsqueeze(1).broadcast_to([P, 4, 4])
            bn = blk.unsqueeze(2).broadcast_to([P, 4, 4])
            gt = stat[:, 16:32].rearrange("p (n m) -> p n m", n=4)
            eq = stat[:, 32:48].rearrange("p (n m) -> p n m", n=4)
            ch.link(dve.tensor_tensor(gt, bm, bn, ALU.is_gt))
            ch.link(dve.tensor_tensor(eq, bm, bn, ALU.is_equal))
            ch.link(dve.tensor_tensor(eq, eq, C("tri").rearrange("p (n m) -> p n m", n=4), ALU.mult))
            ch.link(dve.tensor_tensor(gt, gt, eq, ALU.add))
            ch.link(dve.tensor_reduce(stat[:, 12:16], gt, AX.X, ALU.add))
            ch.link(dve.tensor_scalar(stat[:, 12:16], stat[:, 12:16], 2.5, -BIG, ALU.is_gt, ALU.mult))
            ch.link(dve.tensor_scalar(stat[:, 12:16], stat[:, 12:16], C("rowA"), None, ALU.mult))
            pen = stat[:, 12:16].unsqueeze(2).broadcast_to([P, 4, 2])
            ch.link(dve.tensor_tensor(stat[:, 48:56].rearrange("p (b g) -> p b g", b=4), C("pageslope").rearrange("p (b g) -> p b g", b=4), pen, ALU.add))
            for g in range(NPG):
                ins = dve.scalar_tensor_tensor(out=prob[:, 128 * g:128 * g + 128], in0=bank[:, 6 + g // 4, 128 * (g % 4):128 * (g % 4) + 128],
                                               scalar=stat[:, 48 + g:49 + g], in1=b0[:, :], op0=ALU.add, op1=ALU.add)
            ch.link(ins)
            ch.link(dve.tensor_reduce(stat[:, 2:3], prob[:, :], AX.X, ALU.max))
            ch.link(dve.tensor_tensor(stat[:, 2:3], stat[:, 2:3], ncur[:, :], ALU.max))
            dve.tensor_scalar(stat[:, 3:4], stat[:, 2:3], -1.0, None, ALU.mult).then_inc(s_logit, 1)
            lo(W_BR, 0)
            lo(W_BR, 1)
            v.wait_ge(s_prob, 1)
            ch.link(dve.tensor_tensor(stat[:, 6:7], stat[:, 4:5], stat[:, 5:6], ALU.add))
            ch.link(dve.reciprocal(stat[:, 6:7], stat[:, 6:7]))
            ch.link(dve.tensor_tensor(stat[:, 6:7], stat[:, 6:7], misc[:, 7:8], ALU.mult))
            dve.tensor_scalar(prob[:, :], prob[:, :], stat[:, 6:7], None, ALU.mult).then_inc(s_pscaled, 1)
            ch.link(dve.tensor_tensor(stat[:, 5:6], stat[:, 5:6], stat[:, 6:7], ALU.mult))
            dve.tensor_scalar(ecur[:, :], C("perm"), stat[:, 5:6], None, ALU.mult).then_inc(s_diag, 1)
            ch.link(dve.memset(dcur[:, :], 0.0))
            dve.memset(sall[:, :, P:RW], 0.0).then_inc(s_diag, 1)
            lo(W_BR + 1, 0)
            lo(W_BR + 1, 1)

            def prompt_logits(c):
                for h in range(2):
                    j = 2 * c + h
                    v.wait_ge(s_psc, j + 1)
                    o = 16 * h + 16
                    if c:
                        v.wait_ge(s_ppT, min(2 * c, 8) + max(c - 4, 0))
                    ch.link(dve.scalar_tensor_tensor(out=plog[h][:, :], in0=C("dist"), scalar=-slope_of_row(j), in1=bank[:, h, 0:384], op0=ALU.mult, op1=ALU.add))
                    ch.link(dve.tensor_reduce(stat[:, o:o + 3], plog[h][:, :].rearrange("p (a n) -> p a n", n=128), AX.X, ALU.max))
                    ch.link(dve.tensor_tensor(stat[:, o + 1:o + 2], stat[:, o + 1:o + 2], stat[:, o + 2:o + 3], ALU.max))
                    dve.tensor_scalar(stat[:, o + 3:o + 5], stat[:, o:o + 2], -1.0, None, ALU.mult).then_inc(s_plog, 1)

            prompt_logits(0)
            for c in range(KC):
                for h in range(2):
                    j = 2 * c + h
                    o = 16 * h + 16
                    v.wait_ge(s_pexp, j + 1)
                    ch.link(dve.reciprocal(stat[:, o + 8:o + 10], stat[:, o + 5:o + 7]))
                    if c >= 4 and h == 1:
                        ch.link(dve.tensor_scalar(stat[:, o + 8:o + 10], stat[:, o + 8:o + 10], misc[:, 6:7], None, ALU.mult))
                        v.wait_ge(s_pscale, j)
                    for seg, (e0, e1) in enumerate(((0, 128), (128, 384))):
                        pr = plog[h][:, e0:e1]
                        r_ = stat[:, o + 8 + seg:o + 9 + seg]
                        if c >= 4 and h == 1:
                            ins = dve.scalar_tensor_tensor(out=plog[0][:, e0:e1], in0=pr, scalar=r_, in1=plog[0][:, e0:e1], op0=ALU.mult, op1=ALU.add)
                        else:
                            ins = dve.tensor_scalar(pr, pr, r_, None, ALU.mult)
                    ins.then_inc(s_pscale, 1)
                v.wait_ge(s_pvd, c + 1)
                if c:
                    v.wait_ge(s_ext, c)
                dve.tensor_tensor(om[:, 0, :], bank[:, 4, :], C("maskA"), ALU.mult)
                dve.tensor_tensor(om[:, 1, :], bank[:, 5, :], C("maskB"), ALU.mult).then_inc(s_om, 1)
                if c + 1 < KC:
                    prompt_logits(c + 1)
            v.wait_ge(s_ext, TS)
            dve.tensor_copy(work[:, :, TP:T], bank[:, 3, 0:64].rearrange("p (c s) -> p c s", c=KC)).then_inc(s_samp, 1)
            v.wait_ge(s_pout, KC)
            v.wait_ge(s_ohi, 1)
            dve.tensor_tensor(hlo[:, 0:4, :], work[:, 0:4, :], hhi[:, 0:4, :].bitcast(F32), ALU.subtract).then_inc(s_olo, 1)
            v.wait_ge(s_osum, 1)
            ch.link(dve.tensor_scalar(osq[:, :, :], bank[:, 4:8, 0:T], 1.0 / P, EPS, ALU.mult, ALU.add))
            dve.reciprocal(osq[:, :, :], osq[:, :, :]).then_inc(s_ovar, 1)
            v.wait_ge(s_orstd, 1)
            dve.scalar_tensor_tensor(out=work[:, 4:8, :], in0=work[:, 4:8, :], scalar=misc[:, 12:13], in1=osq[:, :, :], op0=ALU.mult, op1=ALU.mult).then_inc(s_o, 1)
            v.wait_ge(s_ohi, 2)
            v.wait_ge(s_o, 1)
            dve.tensor_tensor(hlo[:, 4:8, :], work[:, 4:8, :], hhi[:, 4:8, :].bitcast(F32), ALU.subtract).then_inc(s_olo, 1)
            for q in range(4):
                ab, half = q // 2, q % 2
                for m in range(4 + 2 * q, 6 + 2 * q):
                    if m < 10:
                        lo(W_BR + m // 2, m % 2)
                v.wait_ge(s_gemm, half_done(W_BR + q, 1))
                if q == 0:
                    v.wait_ge(s_sig, TS)
                if q == 3:
                    v.wait_ge(s_sigend, 1)
                g = gT[:, 8 * ab + 4 * half:8 * ab + 4 * half + 4, :]
                ins = dve.tensor_tensor(g, bank[:, 4 * half:4 * half + 4, 0:T], g, ALU.mult)
                if ab == 0:
                    ins.then_inc(s_turned_g, 1)
                else:
                    ch.link(ins)
                    ga = gT[:, 4 * half:4 * half + 4, :]
                    dve.tensor_tensor(ga, ga, g, ALU.add).then_inc(s_mix, 1)
            for half in range(2):
                v.wait_ge(s_ahi, NPAIR + half + 1)
                v.wait_ge(s_mix, half + 1)
                dve.tensor_tensor(alo[:, 4 * half:4 * half + 4, :], gT[:, 4 * half:4 * half + 4, :], ahi[:, 4 * half:4 * half + 4, :].bitcast(F32),
                                  ALU.subtract).then_inc(s_alo, 1)
            for m in range(2, 11):
                if m in (6, 8, 10):
                    cb = (m - 6) // 2
                    v.wait_ge(s_gemm, half_done(W_OUT + cb, 1))
                    x_update(2 * (cb % 2), 2 * cb, 5)
                lo(W_OUT + m // 2, m % 2)
            v.wait_ge(s_gemm, half_done(W_OUT + 3, 1))
            x_update(2, 6, 5)
            variance(2)
            norm_rows(2)
            with v.Fori(0, NPAIR // 2) as i:
                ff_turn(2 * i, W_FF2, NPAIR, NPAIR + 2, 0, i, False)
                ff_turn(2 * i + 1, W_FF2, NPAIR, NPAIR + 2, 1, i, False)
            ff_turn(NPAIR - 1, W_FF2, NPAIR, NPAIR + 2, NPAIR - 1, 0, False)
            down(W_DN2, 8, False)

        @block.tensor
        def _(pe):
            mm = nc.tensor.matmul

            def product(b, slot, k, w, col, xh, xl, start, stop):
                wh = whi[slot][:, k * w + col:k * w + col + P]
                wl = wlo[slot][:, k * w + col:k * w + col + P]
                out = bank[:, b, 0:T]
                mm(out, wh, xh, start=start, stop=False)
                mm(out, wh, xl, start=False, stop=False)
                return mm(out, wl, xh, start=False, stop=stop)

            def block_half(b, n, parity, half, xh, xl, nk=KC, w=256, k0=0, first=True, last=True, chunks=None):
                pe.wait_ge(s_lo, half_done(n, half))
                per = w // P // 2
                for t in range(half * per, half * per + per):
                    for k in range(nk):
                        if chunks and t == 0:
                            pe.wait_ge(chunks[0], chunks[1](k))
                        ins = product(b + t, parity, k, w, t * P, xh[:, k0 + k, :], xl[:, k0 + k, :], first and k == 0, last and k == nk - 1)
                ins.then_inc(s_gemm, 1)

            def ada(c, key_c=None, d=0):
                key_c = c if key_c is None else key_c
                if not (isinstance(c, int) and c == 0):
                    pe.wait_ge(s_adarow, c)
                for half in range(2):
                    key = ("ada", key_c, half)
                    s = slot_of(key)
                    pe.wait_ge(s_raw[s], landed(key) + 16 * d)
                    for j in range(4):
                        ins = mm(bank[32 * j:32 * j + 32, 4, :], csilu[:, 4 * half + j, :], raw[s][:, 512 * j:512 * j + 512], start=(half == 0), stop=(half == 1))
                ins.then_inc(s_ada, 1)

            def ada_turn(c):
                pe.wait_ge(s_adarow, c + 1)
                if not (isinstance(c, int) and c == 0):
                    pe.wait_ge(s_mod, c)
                for t in range(4):
                    ins = mm(bank[:, 5, 9 * t:9 * t + 9], adarow[:, P * t:P * t + P], C("sel9"), start=True, stop=True)
                ins.then_inc(s_sel, 1)

            def norm_sum(t, cb):
                pe.wait_ge(s_sq, 4 * t + cb + 1)
                for c in (2 * cb, 2 * cb + 1):
                    ins = mm(bank[:, 6, 0:T], C("ones"), work[:, c, :], start=(c == 0), stop=(c == KC - 1))
                if cb == 3:
                    ins.then_inc(s_ssum, 1)

            pe.wait_ge(s_const, 16)
            pe.wait_ge(s_rows, 16)
            pe.wait_ge(s_crow, 16)
            nc.tensor.transpose(bank[:, 7, 0:NROWS], rows[:, :], ident[0:NROWS, 0:NROWS])
            nc.tensor.transpose(bank[:, 6, 0:72], crow[:, :], ident[0:72, 0:72]).then_inc(s_parT, 1)
            pe.wait_ge(s_x, 32)
            for r2 in range(2):
                if r2:
                    pe.wait_ge(s_xfirst, 1)
                for q in range(4):
                    c = 4 * r2 + q
                    for tt in range(2):
                        nc.tensor.transpose(bank[:, q, P * tt:P * tt + P], xtok[:, tt, P * c:P * c + P], ident)
                    ins = nc.tensor.transpose(bank[:, q, TP:T], xtoks[:, P * c:P * c + P], ident[0:TS, 0:TS])
                ins.then_inc(s_xT, 1)
            pe.wait_ge(s_par, 2)
            pe.wait_ge(s_csilu, 1)
            mm(bank[:, 6, 0:2], C("ones"), misc[:, 2:4], start=True, stop=True).then_inc(s_lamsum, 1)
            pe.wait_ge(s_lamexp, 1)
            ada(0)
            for cb in range(4):
                norm_sum(0, cb)
            ada_turn(0)
            for c in range(1, ADA_PRO):
                ada(c)
                ada_turn(c)

            def ff_gate(i, n, pairs, chunks=None):
                if not (isinstance(i, int) and i + pairs == 0):
                    pe.wait_ge(s_sil, pairs + i)
                for t in range(2):
                    block_half(0, n, 0, t, hhi, hlo, chunks=chunks)

            def ff_up(i, n, pairs):
                if not (isinstance(i, int) and i + pairs == 0):
                    pe.wait_ge(s_act, pairs + i)
                for t in range(2):
                    block_half(2, n, 1, t, hhi, hlo)

            def ff1_turn(i, key_i, d, chunks=None):
                ff_gate(i, W_FF1 + 2 * i, 0, chunks)
                ada(ADA_PRO + i, ADA_PRO + key_i, d)
                ff_up(i, W_FF1 + 2 * i + 1, 0)
                ada_turn(ADA_PRO + i)

            ff1_turn(0, 0, 0, (s_hlo, lambda k: k + 1))
            with pe.Fori(1, NPAIR) as i:
                ff1_turn(i, 1, i - 1)

            def down(first, pairs, alos, xups, with_ada):
                for cb in range(4):
                    for third in range(3):
                        n = first + 3 * cb + third
                        if cb == 0:
                            pe.wait_ge(s_alo, alos - NPAIR + (4, 8, 11)[third])
                        if third == 0:
                            if cb == 0:
                                pe.wait_ge(s_sil, pairs)
                            elif cb == 1:
                                pe.wait_ge(s_act, pairs)
                            else:
                                pe.wait_ge(s_xup, xups + cb - 1)
                        nk = min(FC - 8 * third, 8)
                        for t in range(2):
                            block_half(2 * (cb % 2), n, n % 2, t, ahi, alo, nk=nk, k0=8 * third, first=(third == 0), last=(third == 2))
                        u = 3 * cb + third
                        if with_ada and u in (3, 7):
                            ada(ADA_PRO + NPAIR + u // 4)
                        if with_ada and u in (5, 9):
                            ada_turn(ADA_PRO + NPAIR + u // 8)
                        if with_ada and cb and third == 1:
                            norm_sum(1, cb - 1)
                        if not with_ada and cb and third == 1:
                            y_turn(cb - 1)
                if with_ada:
                    ada(ADAC - 1)
                    norm_sum(1, 3)
                    ada_turn(ADAC - 1)
                else:
                    y_turn(3)

            def y_turn(cb):
                pe.wait_ge(s_xup, 8 + cb + 1)
                if cb:
                    pe.wait_ge(s_ys, 2 * cb)
                for t in range(2):
                    for tt in range(2):
                        nc.tensor.transpose(bank[:, 4, 256 * tt + P * t:256 * tt + P * t + P], x[:, 2 * cb + t, P * tt:P * tt + P], ident)
                    ins = nc.tensor.transpose(bank[0:TS, 5, P * t:P * t + P], x[:, 2 * cb + t, TP:T], ident)
                ins.then_inc(s_yT, 1)

            down(W_DN1, NPAIR, NPAIR, 0, True)

            nk = tk = 0
            for u in range(13):
                n = W_QKV + u
                if u < 12:
                    if u >= 2:
                        pe.wait_ge(s_proj, u - 1)
                    else:
                        pe.wait_ge(s_xup, 4)
                    block_half(2 * (u % 2), n, n % 2, 0, hhi, hlo, chunks=(s_hlo, lambda k: KC + k + 1) if u == 0 else None)
                w = u - 1
                kind = w % 6 // 2
                if u > 0 and kind < 2:
                    pe.wait_ge(s_proj, w + 1)
                    if nk:
                        pe.wait_ge(s_nvar, nk)
                    for t in range(2):
                        ins = mm(bank[:, 6 + t, 0:T], C("blockdiag"), sqb[:, t, :], start=True, stop=True)
                    ins.then_inc(s_nsum, 1)
                    nk += 1
                if u < 12:
                    block_half(2 * (u % 2), n, n % 2, 1, hhi, hlo)
                if u > 0 and kind > 0:
                    ab, p = w // 6, w % 2
                    if kind == 1:
                        pe.wait_ge(s_qk, nk)
                    else:
                        pe.wait_ge(s_proj, w + 1)
                    if tk:
                        pe.wait_ge(s_tok, 2 * tk)
                    else:
                        pe.wait_ge(s_mod, ADAC)
                    for t in range(2):
                        src = kT[:, 4 * ab + 2 * p + t, :] if kind == 1 else vT[:, t, :]
                        for tt in range(2):
                            nc.tensor.transpose(bank[:, 4, 256 * tt + P * t:256 * tt + P * t + P], src[:, P * tt:P * tt + P], ident)
                        ins = nc.tensor.transpose(bank[0:TS, 5, P * t:P * t + P], src[:, TP:T], ident)
                    ins.then_inc(s_turn, 1)
                    tk += 1

            pe.wait_ge(s_ecur, 1)
            mm(bank[:, 7, 0:1], ev0[:, :], C("ones", 0, 1), start=True, stop=True).then_inc(s_cur, 1)

            def chunk_turn(s, g):
                for ab in range(2):
                    use = 2 * s + g // 4
                    m = chunk_of(ab, g)
                    if g % 4 == 0:
                        pe.wait_ge(s_kv[ab][use % KVS], kv_landed(use))
                    if NPG * s + g >= 2:
                        pe.wait_ge(s_kTs[ab], NPG * s + g - 1)
                    b = 2 + 2 * (g % 2) + ab
                    for q in range(4):
                        ins = nc.tensor.transpose(bank[:, b, P * q:P * q + P], kv_slot(ab, use)[:, q, P * m:P * m + P], ident)
                    ins.then_inc(s_kTp[ab], 1)

            def chunk_scores(s, g):
                pe.wait_ge(s_qpad, s + 1)
                for ab in range(2):
                    m = chunk_of(ab, g)
                    at_ = 30 - (4 * s + 2 * ab)
                    pe.wait_ge(s_kTs[ab], NPG * s + g + 1)
                    mm(bank[32 * m:32 * m + 32, 6 + g // 4, :], qpad[s % 2][:, 4 * ab + m, at_:at_ + 32], kTs[ab][g % 2][:, :],
                       start=(s == 0 and g % 4 < 2), stop=(s == TS - 1 and g % 4 >= 2)).then_inc(s_kS[ab], 1)

            def gate_block(s):
                if s == 0:
                    pe.wait_ge(s_proj, 12)
                else:
                    pe.wait_ge(s_sig, s if s < 7 else 6)
                for t in range(2):
                    block_half(2 if s == 7 else 0, W_GATE + s, (W_GATE + s) % 2, t, hhi, hlo)

            pe.wait_ge(s_proj, 12)
            pe.wait_ge(s_tok, 16)
            pe.wait_ge(s_nvar, nk)
            chunk_turn(0, 0)
            chunk_turn(0, 1)
            pe.wait_ge(s_ncur, 1)
            for s in range(TS):
                for g in range(0, NPG, 2):
                    for ahead in (g + 2, g + 3):
                        if ahead < NPG:
                            chunk_turn(s, ahead)
                        elif s + 1 < TS:
                            chunk_turn(s + 1, ahead - NPG)
                    chunk_scores(s, g)
                    chunk_scores(s, g + 1)
                if s < 6:
                    gate_block(s)

            gate_block(6)
            gate_block(7)

            def prompt_scores(c):
                for h in range(2):
                    r0, r1 = 64 * h, 64 * h + 64
                    mm(bank[:, h, 0:128], qT[r0:r1, c, 0:128], kT[r0:r1, c, 0:128], start=True, stop=True)
                    mm(bank[:, h, 128:384], qT[r0:r1, c, 128:256], kT[r0:r1, c, 0:256], start=True, stop=True).then_inc(s_psc, 1)

            pe.wait_ge(s_sig, 7)
            prompt_scores(0)
            pe.wait_ge(s_pscaled, 1)
            for g in range(NPG):
                ins = mm(bank[:, 6 + g // 4, P * (g % 4):P * (g % 4) + P], prob[:, P * g:P * g + P], C("perm"), start=True, stop=True)
            ins.then_inc(s_pT, 1)
            pe.wait_ge(s_diag, 2)
            pe.wait_ge(s_sig, TS)
            mm(bank[0:TS, 3, 0:P], C("sel8"), ecur[:, :], start=True, stop=True).then_inc(s_dps, 1)

            npp = 0
            pe.wait_ge(s_pTs, 1)
            pe.wait_ge(s_dcur, 1)
            for c in range(KC):
                if c:
                    pe.wait_ge(s_om, c)
                for half in range(2):
                    for ab in range(2):
                        use = 16 + 2 * c + half
                        pe.wait_ge(s_kv[ab][use % KVS], kv_landed(use))
                        r0 = 16 * c + 8 * ab
                        for q in range(4):
                            ins = mm(bank[32 * q:32 * q + 32, 4 + ab, :], sall[:, 4 * half + q, r0:r0 + 32], kv_slot(ab, use)[:, q, :],
                                     start=(half == 0), stop=(half == 1 and q > 0))
                        ins.then_inc(s_pv, 1)
                for ab in range(2):
                    r0 = 16 * c + 8 * ab
                    ins = mm(bank[0:32, 4 + ab, :], dcur[:, r0:r0 + 32], vtoks[:, 512 * ab:512 * ab + 512], start=False, stop=True)
                ins.then_inc(s_pvd, 1)
                for h in range(2 if c < 4 else 1):
                    pe.wait_ge(s_pscale, 2 * c + (h + 1 if c < 4 else 2))
                    if npp:
                        pe.wait_ge(s_pps, npp)
                    for e in range(3):
                        ins = nc.tensor.transpose(bank[:, 6 + h, P * e:P * e + P], plog[h][:, P * e:P * e + P], ident)
                    ins.then_inc(s_ppT, 1)
                    npp += 1
                if c + 1 < KC:
                    pe.wait_ge(s_plog, 2 * c + 2)
                    prompt_scores(c + 1)
                pe.wait_ge(s_om, c + 1)
                for f in range(KC):
                    ins = mm(bank[:, 3, TS * f + c:TS * f + c + 1], om[:, f // 4, P * (f % 4):P * (f % 4) + P], C("ones", 0, 1), start=True, stop=True)
                ins.then_inc(s_ext, 1)
                pe.wait_ge(s_pps, npp)
                if c:
                    pe.wait_ge(s_pout, c)
                for h in range(2 if c < 4 else 1):
                    wd = 64 if c < 4 else 128
                    v0 = P * c + 64 * h
                    out = bank[64 * h:64 * h + wd, 2, :]
                    mm(out[:, 0:TP], vtok[:, 0, v0:v0 + wd], pts[h][:, 0:256], start=True, stop=False)
                    ins = mm(out[:, 128:TP], vtok[:, 1, v0:v0 + wd], pts[h][:, 256:384], start=False, stop=True)
                ins.then_inc(s_po, 1)
            pe.wait_ge(s_osq, 1)
            for q in range(4):
                ins = mm(bank[:, 4 + q, 0:T], C("ones"), osq[:, q, :], start=True, stop=True)
            ins.then_inc(s_osum, 1)

            for q in range(4):
                n = W_BR + q
                ab, half = q // 2, q % 2
                pe.wait_ge(s_olo, ab + 1)
                if q == 1:
                    pe.wait_ge(s_ovar, 1)
                if q >= 2:
                    pe.wait_ge(s_turned_g, q - 1)
                for t in range(2):
                    block_half(4 * half, n, n % 2, t, hhi, hlo, nk=4, w=512, k0=4 * ab)
            for cb in range(4):
                n = W_OUT + cb
                if cb == 0:
                    pe.wait_ge(s_mix, 1)
                if cb >= 2:
                    pe.wait_ge(s_xup, 4 + cb - 1)
                for t in range(2):
                    block_half(2 * (cb % 2), n, n % 2, t, ahi, alo, chunks=(s_alo, lambda k: NPAIR + 1 + k // 4) if cb == 0 else None)
                    if t == 0 and cb >= 2:
                        norm_sum(2, cb - 2)
            norm_sum(2, 2)
            norm_sum(2, 3)
            ff_gate(0, W_FF2, NPAIR, (s_hlo, lambda k: 2 * KC + k + 1))
            ff_up(0, W_FF2 + 1, NPAIR)
            with pe.Fori(0, NPAIR // 2) as i:
                for q in range(1, 3):
                    j = 2 * i + q
                    ff_gate(j, W_FF2 + 2 * j, NPAIR)
                    ff_up(j, W_FF2 + 2 * j + 1, NPAIR)
            down(W_DN2, 2 * NPAIR, 2 * NPAIR + 2, 8, False)



OUTS = [("y_prompt", (1, TP, D)), ("y_sample", (TS, 1, D)),
        ("k_moba_prompt", (1, 1, TP, 8, 64)), ("v_moba_prompt", (1, 1, TP, 8, 64)),
        ("k_diff_prompt", (1, 1, TP, 4, 128)), ("v_diff_prompt", (1, 1, TP, 4, 128)),
        ("k_moba_sample", (1, TS, 1, 8, 64)), ("v_moba_sample", (1, TS, 1, 8, 64)),
        ("k_diff_sample", (1, TS, 1, 4, 128)), ("v_diff_sample", (1, TS, 1, 4, 128))]
DIRECT = ["x_prompt", "x_sample", "cache_k_moba", "cache_v_moba", "cache_k_diff", "cache_v_diff", "page_table", "w_ada",
          "ffn1_w_gate", "ffn1_w_up", "ffn1_w_down", "w_in", "w_branch_moba", "w_branch_diff", "w_out",
          "ffn2_w_gate", "ffn2_w_up", "ffn2_w_down"]


def kernel(**inputs):
    import concourse.bacc as bacc
    from concourse.bass_utils import run_bass_kernel_spmd

    g = {k: np.asarray(v) for k, v in inputs.items()}
    arrays = {k: np.ascontiguousarray(g[k]) for k in DIRECT}
    arrays["params"] = np.concatenate([
        g["b_ada"].reshape(72, P), g["norm_ffn1"].reshape(8, P), g["norm_mix"].reshape(8, P), g["norm_ffn2"].reshape(8, P)]
        + [np.concatenate([g[n], g[n]], 1) for n in ("qn_moba", "kn_moba", "qn_diff", "kn_diff")]
        + [g["subln_diff"], np.concatenate([g["lambda_q1"], g["lambda_q2"]], 1), np.concatenate([g["lambda_k1"], g["lambda_k2"]], 1)], 0)
    c9 = np.concatenate([g["c_prompt"], g["c_sample"]], 0)
    arrays["c_rows"] = np.ascontiguousarray(c9.reshape(9, KC, P).transpose(1, 0, 2)).reshape(72, P)
    arrays["consts"] = constants()

    nc = bacc.Bacc("TRN2", target_bir_lowering=False, num_devices=1)
    A = {k: nc.dram_tensor(f"in_{k}", a.shape, mybir.dt.from_np(a.dtype), kind="ExternalInput").ap() for k, a in arrays.items()}
    O = {k: nc.dram_tensor(f"out_{k}", s, F32, kind="ExternalOutput").ap() for k, s in OUTS}
    build(nc, A, O)
    r = run_bass_kernel_spmd(nc, [{f"in_{k}": a for k, a in arrays.items()}], core_ids=[0])
    return tuple(r.results[0][f"out_{k}"] for k, _ in OUTS)
```
